# Optimizing a Trainium2 kernel written in Bass

```python
import jax, jax.numpy as jnp
from jax import lax
import numpy as np
import jax
import jax.numpy as jnp

D_MODEL = 1024
BATCH = 1
SEQ = 256
DEPTH = 2

HEAD_DIM = 64
RET_HEADS = (3 * D_MODEL // 8) // HEAD_DIM
MOBA_HEADS = (3 * D_MODEL // 8) // HEAD_DIM
CONV_GROUPS = (D_MODEL // 4) // HEAD_DIM
RET_WIDTH = RET_HEADS * HEAD_DIM
MOBA_WIDTH = MOBA_HEADS * HEAD_DIM
CONV_WIDTH = CONV_GROUPS * HEAD_DIM
MIX_WIDTH = RET_WIDTH + MOBA_WIDTH + CONV_WIDTH
IN_WIDTH = 4 * RET_WIDTH + 3 * MOBA_WIDTH + 2 * CONV_WIDTH
D_FF = ((8 * D_MODEL // 3 + 255) // 256) * 256
RET_CHUNK = 256
RET_ROT_BASE = 10000.0
MOBA_BLOCK = 256
MOBA_TOPK = 3
MOBA_QBLOCK = 128
ROPE_THETA = 500000.0
ROPE_DIMS = HEAD_DIM // 4
CONV_KERNEL = 31
FFN_RES_WEIGHT = 0.5
EPS = 1e-6
PAD_MULT = 256


def rms_norm(x, g):
    xf = x.astype(jnp.float32)
    y = xf * lax.rsqrt(jnp.mean(xf * xf, -1, keepdims=True) + EPS)
    return (y * g.astype(jnp.float32)).astype(x.dtype)

def swiglu(h, wg, wu, wd):
    return (jax.nn.silu(h @ wg) * (h @ wu)) @ wd

def to_heads(t, n_heads):
    b, s, _ = t.shape
    return t.reshape(b, s, n_heads, HEAD_DIM).transpose(0, 2, 1, 3)

def from_heads(t):
    b, h, s, d = t.shape
    return t.transpose(0, 2, 1, 3).reshape(b, s, h * d)

def rotary(x, pos, inv_freq):
    half = inv_freq.shape[0]
    n_rot = 2 * half
    ang = pos.astype(jnp.float32)[:, None, :, None] * inv_freq
    cos, sin = jnp.cos(ang), jnp.sin(ang)
    xr = x[..., :n_rot].astype(jnp.float32)
    x1, x2 = xr[..., :half], xr[..., half:]
    rot = jnp.concatenate([x1 * cos - x2 * sin, x2 * cos + x1 * sin], -1).astype(x.dtype)
    return jnp.concatenate([rot, x[..., n_rot:]], -1)

def retention(q, k, v):
    b, h, s, d = q.shape
    c = RET_CHUNK
    n = s // c
    log_gamma = jnp.log1p(-jnp.exp2(-5.0 - jnp.arange(h, dtype=jnp.float32)))
    lg = log_gamma[:, None]
    qc = q.reshape(b, h, n, c, d)
    kc = (k * (d ** -0.5)).reshape(b, h, n, c, d)
    vc = v.reshape(b, h, n, c, d)
    idx = jnp.arange(c, dtype=jnp.float32)
    rel = idx[:, None] - idx[None, :]
    decay_in = jnp.where(rel >= 0, jnp.exp(lg[:, :, None] * jnp.maximum(rel, 0.0)), 0.0)
    scores = jnp.einsum('bhncd,bhnmd->bhncm', qc, kc) * decay_in[None, :, None]
    inner = jnp.einsum('bhncm,bhnme->bhnce', scores, vc)
    w_state = jnp.exp(lg * (c - 1 - idx))
    kv = jnp.einsum('bhncd,hc,bhnce->bhnde', kc, w_state, vc)
    chunk_decay = jnp.exp(log_gamma * c).astype(kv.dtype)[None, :, None, None]

    def step(state, kv_i):
        return state * chunk_decay + kv_i, state

    _, prev = lax.scan(step, jnp.zeros((b, h, d, d), kv.dtype), jnp.moveaxis(kv, 2, 0))
    prev = jnp.moveaxis(prev, 0, 2)
    w_cross = jnp.exp(lg * (idx + 1.0))
    cross = jnp.einsum('bhncd,bhnde->bhnce', qc, prev) * w_cross[None, :, None, :, None]
    return (inner + cross).reshape(b, h, s, d)

def moba_attention(q, k, v):
    b, h, s, d = q.shape
    bs = MOBA_BLOCK
    nb = s // bs
    qb = MOBA_QBLOCK
    nq = s // qb
    topk = min(MOBA_TOPK, nb)
    scale = d ** -0.5
    kb = k.reshape(b, h, nb, bs, d)
    vb = v.reshape(b, h, nb, bs, d)
    kmean = jnp.mean(kb.astype(jnp.float32), axis=3)
    b_i = jnp.arange(b)[:, None, None]
    h_i = jnp.arange(h)[None, :, None]
    klocal = jnp.arange(bs)

    def one_qblock(args):
        qblk, qi = args
        qpos = qi * qb + jnp.arange(qb)
        own = (qi * qb) // bs
        gate = jnp.einsum('bhqd,bhnd->bhqn', qblk.astype(jnp.float32), kmean)
        gate = jnp.where(jnp.arange(nb) < own, gate, -jnp.inf)
        _, sel = lax.top_k(gate, topk)
        valid = sel < own
        k_own = lax.dynamic_index_in_dim(kb, own, axis=2, keepdims=False)
        v_own = lax.dynamic_index_in_dim(vb, own, axis=2, keepdims=False)
        s_own = jnp.einsum('bhqd,bhkd->bhqk', qblk, k_own).astype(jnp.float32) * scale
        causal = (own * bs + klocal)[None, :] <= qpos[:, None]
        s_list = [jnp.where(causal, s_own, -jnp.inf)]
        for j in range(topk):
            k_j = kb[b_i, h_i, sel[..., j]]
            s_j = jnp.einsum('bhqd,bhqkd->bhqk', qblk, k_j).astype(jnp.float32) * scale
            s_list.append(jnp.where(valid[..., j, None], s_j, -jnp.inf))
        p = jax.nn.softmax(jnp.concatenate(s_list, -1), axis=-1).astype(v.dtype)
        out = jnp.einsum('bhqk,bhkd->bhqd', p[..., :bs], v_own)
        for j in range(topk):
            v_j = vb[b_i, h_i, sel[..., j]]
            out = out + jnp.einsum('bhqk,bhqkd->bhqd', p[..., (j + 1) * bs:(j + 2) * bs], v_j)
        return out

    qs = jnp.moveaxis(q.reshape(b, h, nq, qb, d), 2, 0)
    outs = lax.map(one_qblock, (qs, jnp.arange(nq)))
    return jnp.moveaxis(outs, 0, 2).reshape(b, h, s, d)

def conv_module(a, gate, w, bias, ln_g, ln_b):
    bsz, s, c = a.shape
    u = a * jax.nn.sigmoid(gate)
    y = lax.conv_general_dilated(u, w[:, None, :], window_strides=(1,), padding=[(CONV_KERNEL - 1, 0)],
                                 dimension_numbers=('NWC', 'WIO', 'NWC'), feature_group_count=c) + bias
    yg = y.reshape(bsz, s, CONV_GROUPS, c // CONV_GROUPS).astype(jnp.float32)
    mu = jnp.mean(yg, -1, keepdims=True)
    var = jnp.mean(jnp.square(yg - mu), -1, keepdims=True)
    yn = ((yg - mu) * lax.rsqrt(var + EPS)).reshape(bsz, s, c) * ln_g.astype(jnp.float32) + ln_b.astype(jnp.float32)
    return jax.nn.silu(yn).astype(a.dtype)

def first_inputs(seed: int = 0) -> dict:
    key = jax.random.key(seed)
    ks = jax.random.split(key, 20)
    f32 = jnp.float32

    def w(k, shape, fan_in):
        return jax.random.normal(k, shape, f32) * (fan_in ** -0.5)

    def gain(k, shape):
        return 1.0 + 0.02 * jax.random.normal(k, shape, f32)

    return {
        "x": jax.random.normal(ks[0], (BATCH, SEQ, D_MODEL), f32),
        "positions": jnp.broadcast_to(jnp.arange(SEQ, dtype=jnp.int32), (BATCH, SEQ)),
        "ffn1_norm": gain(ks[1], (DEPTH, D_MODEL)),
        "ffn1_wg": w(ks[2], (DEPTH, D_MODEL, D_FF), D_MODEL),
        "ffn1_wu": w(ks[3], (DEPTH, D_MODEL, D_FF), D_MODEL),
        "ffn1_wd": w(ks[4], (DEPTH, D_FF, D_MODEL), D_FF),
        "mix_norm": gain(ks[5], (DEPTH, D_MODEL)),
        "w_in": w(ks[6], (DEPTH, D_MODEL, IN_WIDTH), D_MODEL),
        "conv_w": w(ks[7], (DEPTH, CONV_KERNEL, CONV_WIDTH), CONV_KERNEL),
        "conv_b": 0.02 * jax.random.normal(ks[8], (DEPTH, CONV_WIDTH), f32),
        "conv_ln_g": gain(ks[9], (DEPTH, CONV_WIDTH)),
        "conv_ln_b": 0.02 * jax.random.normal(ks[10], (DEPTH, CONV_WIDTH), f32),
        "w_out": w(ks[11], (DEPTH, MIX_WIDTH, D_MODEL), MIX_WIDTH),
        "ffn2_norm": gain(ks[12], (DEPTH, D_MODEL)),
        "ffn2_wg": w(ks[13], (DEPTH, D_MODEL, D_FF), D_MODEL),
        "ffn2_wu": w(ks[14], (DEPTH, D_MODEL, D_FF), D_MODEL),
        "ffn2_wd": w(ks[15], (DEPTH, D_FF, D_MODEL), D_FF),
        "final_norm": gain(ks[16], (D_MODEL,)),
    }

def first_block(x, positions, ffn1_norm, ffn1_wg, ffn1_wu, ffn1_wd, mix_norm, w_in, conv_w, conv_b,
              conv_ln_g, conv_ln_b, w_out, ffn2_norm, ffn2_wg, ffn2_wu, ffn2_wd, final_norm):
    s = x.shape[1]
    s_pad = ((s + PAD_MULT - 1) // PAD_MULT) * PAD_MULT
    pad = s_pad - s
    pos = jnp.pad(positions, ((0, 0), (0, pad)))
    half_ret = HEAD_DIM // 2
    ret_inv = RET_ROT_BASE ** (-jnp.linspace(0.0, 1.0, half_ret, dtype=jnp.float32))
    half_rope = ROPE_DIMS // 2
    rope_inv = ROPE_THETA ** (-jnp.arange(half_rope, dtype=jnp.float32) / half_rope)
    sizes = [RET_WIDTH] * 4 + [MOBA_WIDTH] * 3 + [CONV_WIDTH] * 2
    cuts = [int(c) for c in np.cumsum(sizes)[:-1]]

    for l in range(DEPTH):
        h = rms_norm(x, ffn1_norm[l])
        x = x + FFN_RES_WEIGHT * swiglu(h, ffn1_wg[l], ffn1_wu[l], ffn1_wd[l])

        h = rms_norm(x, mix_norm[l])
        z = jnp.pad(h @ w_in[l], ((0, 0), (0, pad), (0, 0)))
        rq, rk, rv, rg, mq, mk, mv, ca, cg = jnp.split(z, cuts, axis=-1)

        rq = rotary(to_heads(rq, RET_HEADS), pos, ret_inv)
        rk = rotary(to_heads(rk, RET_HEADS), pos, ret_inv)
        y_ret = retention(rq, rk, to_heads(rv, RET_HEADS)).astype(jnp.float32)
        y_ret = y_ret * lax.rsqrt(jnp.mean(y_ret * y_ret, -1, keepdims=True) + EPS)
        y_ret = jax.nn.silu(rg) * from_heads(y_ret).astype(rg.dtype)

        mq = rotary(to_heads(mq, MOBA_HEADS), pos, rope_inv)
        mk = rotary(to_heads(mk, MOBA_HEADS), pos, rope_inv)
        y_moba = from_heads(moba_attention(mq, mk, to_heads(mv, MOBA_HEADS)))

        y_conv = conv_module(ca, cg, conv_w[l], conv_b[l], conv_ln_g[l], conv_ln_b[l])

        mix = jnp.concatenate([y_ret, y_moba, y_conv], axis=-1)[:, :s]
        x = x + mix @ w_out[l]

        h = rms_norm(x, ffn2_norm[l])
        x = x + FFN_RES_WEIGHT * swiglu(h, ffn2_wg[l], ffn2_wu[l], ffn2_wd[l])

    return rms_norm(x, final_norm)


ROPE_DIM = HEAD_DIM // 4
Q_BLOCK = 128
NEG_INF = -1e30
RMS_EPS = 1e-6

NSA_HEADS = 4
NSA_CMP_LEN = 32
NSA_CMP_STRIDE = 16
NSA_CMP_HIDDEN = 128
NSA_SEL_LEN = 64
NSA_SEL_TOPK = 16
NSA_WINDOW = 512
NSA_FORCE_SCORE = 1e4

DIL_PATTERNS = ((128, 1), (512, 4), (2048, 16))
DIL_HEADS_PER_GROUP = 2
DIL_HEADS = DIL_HEADS_PER_GROUP * len(DIL_PATTERNS)

FOX_HEADS = 6

D_FF_2 = 2816

NSA_Q_W = NSA_HEADS * HEAD_DIM
NSA_KV_W = 6 * HEAD_DIM
NSA_GATE_W = 3 * NSA_HEADS
DIL_W = DIL_HEADS * HEAD_DIM
DIL_OUT_W = DIL_HEADS_PER_GROUP * HEAD_DIM
FOX_W = FOX_HEADS * HEAD_DIM
IN_WIDTHS = (NSA_Q_W, NSA_KV_W, NSA_GATE_W, 3 * DIL_W, 3 * FOX_W, FOX_HEADS, 3 * D_MODEL)
IN_COLS = sum(IN_WIDTHS)


def _split_cols(x, widths):
    offsets = [int(o) for o in np.cumsum(widths)[:-1]]
    return jnp.split(x, offsets, axis=-1)

def _rms_norm(x, g):
    xf = x.astype(jnp.float32)
    y = xf * lax.rsqrt(jnp.mean(xf * xf, axis=-1, keepdims=True) + RMS_EPS)
    return (y * g.astype(jnp.float32)).astype(x.dtype)

def _modulate(x, shift, scale):
    return x * (1.0 + scale) + shift

def _swiglu(x, w_in, w_out):
    gate, up = jnp.split(x @ w_in, 2, axis=-1)
    return (jax.nn.silu(gate) * up) @ w_out

def _rope_tables(seq_len):
    inv_freq = ROPE_THETA ** (-jnp.arange(0, ROPE_DIM, 2, dtype=jnp.float32) / ROPE_DIM)
    ang = jnp.arange(seq_len, dtype=jnp.float32)[:, None] * inv_freq[None, :]
    return jnp.cos(ang), jnp.sin(ang)

def _partial_rope(x, cos, sin):
    half = ROPE_DIM // 2
    c = cos[None, :, None, :]
    s = sin[None, :, None, :]
    x1 = x[..., :half].astype(jnp.float32)
    x2 = x[..., half:ROPE_DIM].astype(jnp.float32)
    rot = jnp.concatenate([x1 * c - x2 * s, x2 * c + x1 * s], axis=-1).astype(x.dtype)
    return jnp.concatenate([rot, x[..., ROPE_DIM:]], axis=-1)

def _masked_softmax(s, mask):
    s = jnp.where(mask, s, NEG_INF)
    m = jnp.max(s, axis=-1, keepdims=True)
    e = jnp.where(mask, jnp.exp(s - m), 0.0)
    den = jnp.sum(e, axis=-1, keepdims=True)
    den = jnp.where(den > 0, den, 1.0)
    return e / den, m + jnp.log(den)

def _nsa_attention(q, k_cmp, v_cmp, k_sel, v_sel, k_win, v_win, gate_logits,
                   cmp_pe, cmp_w1, cmp_w2):
    B, S = q.shape[0], q.shape[1]
    scale = HEAD_DIM ** -0.5
    n_cmp = (S - NSA_CMP_LEN) // NSA_CMP_STRIDE + 1
    cmp_start = np.arange(n_cmp) * NSA_CMP_STRIDE
    cmp_idx = cmp_start[:, None] + np.arange(NSA_CMP_LEN)[None, :]

    def compress(t, j):
        blk = t[:, cmp_idx] + cmp_pe[j]
        hid = jax.nn.silu(blk.reshape(B, n_cmp, NSA_CMP_LEN * HEAD_DIM) @ cmp_w1[j])
        return hid @ cmp_w2[j]

    kc = compress(k_cmp, 0)
    vc = compress(v_cmp, 1)
    cmp_end = jnp.asarray(cmp_start + NSA_CMP_LEN - 1)
    n_sel = S // NSA_SEL_LEN
    sel_start = np.arange(n_sel) * NSA_SEL_LEN
    ov = np.minimum(cmp_start[:, None] + NSA_CMP_LEN, sel_start[None, :] + NSA_SEL_LEN) \
        - np.maximum(cmp_start[:, None], sel_start[None, :])
    overlap = jnp.asarray(np.clip(ov, 0, None) / NSA_CMP_LEN, dtype=jnp.float32)
    top_k = min(NSA_SEL_TOPK, n_sel)
    sel_ids = jnp.arange(n_sel)
    kw_pad = jnp.pad(k_win, ((0, 0), (NSA_WINDOW, 0), (0, 0)))
    vw_pad = jnp.pad(v_win, ((0, 0), (NSA_WINDOW, 0), (0, 0)))
    win_len = NSA_WINDOW + Q_BLOCK
    gather = jax.vmap(lambda a, i: a[i])

    def block(qb):
        q0 = qb * Q_BLOCK
        t = q0 + jnp.arange(Q_BLOCK)
        qblk = lax.dynamic_slice_in_dim(q, q0, Q_BLOCK, axis=1)
        s = jnp.einsum('bqhd,bnd->bhqn', qblk, kc).astype(jnp.float32) * scale
        p_cmp, _ = _masked_softmax(s, cmp_end[None, :] <= t[:, None])
        o_cmp = jnp.einsum('bhqn,bnd->bqhd', p_cmp.astype(vc.dtype), vc)
        imp = jnp.einsum('bhqn,nj->bqj', p_cmp, overlap)
        valid = (sel_ids[None, :] * NSA_SEL_LEN) <= t[:, None]
        forced = (sel_ids[None, :] == (t // NSA_SEL_LEN)[:, None]) | (sel_ids[None, :] == 0)
        imp = jnp.where(forced, NSA_FORCE_SCORE, jnp.where(valid, imp, -1.0))
        _, blk_idx = lax.top_k(imp, top_k)
        tok = (blk_idx[..., None] * NSA_SEL_LEN + jnp.arange(NSA_SEL_LEN)).reshape(B, Q_BLOCK * top_k * NSA_SEL_LEN)
        ks = gather(k_sel, tok).reshape(B, Q_BLOCK, top_k * NSA_SEL_LEN, HEAD_DIM)
        vs = gather(v_sel, tok).reshape(B, Q_BLOCK, top_k * NSA_SEL_LEN, HEAD_DIM)
        s = jnp.einsum('bqhd,bqkd->bhqk', qblk, ks).astype(jnp.float32) * scale
        smask = (tok.reshape(B, Q_BLOCK, top_k * NSA_SEL_LEN) <= t[None, :, None])[:, None]
        p, _ = _masked_softmax(s, smask)
        o_sel = jnp.einsum('bhqk,bqkd->bqhd', p.astype(vs.dtype), vs)
        kw = lax.dynamic_slice_in_dim(kw_pad, q0, win_len, axis=1)
        vw = lax.dynamic_slice_in_dim(vw_pad, q0, win_len, axis=1)
        kpos = q0 - NSA_WINDOW + jnp.arange(win_len)
        wmask = (kpos[None, :] <= t[:, None]) & (kpos[None, :] > t[:, None] - NSA_WINDOW) & (kpos[None, :] >= 0)
        s = jnp.einsum('bqhd,bkd->bhqk', qblk, kw).astype(jnp.float32) * scale
        p, _ = _masked_softmax(s, wmask)
        o_win = jnp.einsum('bhqk,bkd->bqhd', p.astype(vw.dtype), vw)
        g = jax.nn.sigmoid(lax.dynamic_slice_in_dim(gate_logits, q0, Q_BLOCK, axis=1).astype(jnp.float32)).astype(q.dtype)
        return g[..., 0:1] * o_cmp + g[..., 1:2] * o_sel + g[..., 2:3] * o_win

    out = lax.map(block, jnp.arange(S // Q_BLOCK))
    return out.transpose(1, 0, 2, 3, 4).reshape(B, S, NSA_Q_W)

def _dilated_attention(q, k, v):
    B, S = q.shape[0], q.shape[1]
    scale = HEAD_DIM ** -0.5
    hpg = DIL_HEADS_PER_GROUP
    qg_all = [q[:, :, g * hpg:(g + 1) * hpg] for g in range(len(DIL_PATTERNS))]
    kg_all = [k[:, :, g * hpg:(g + 1) * hpg] for g in range(len(DIL_PATTERNS))]
    vg_all = [v[:, :, g * hpg:(g + 1) * hpg] for g in range(len(DIL_PATTERNS))]

    def block(qb):
        q0 = qb * Q_BLOCK
        t = q0 + jnp.arange(Q_BLOCK)
        outs, lses = [], []
        for g, (window, dil) in enumerate(DIL_PATTERNS):
            qg = lax.dynamic_slice_in_dim(qg_all[g], q0, Q_BLOCK, axis=1)
            pos = t[:, None] - dil * jnp.arange(window // dil + 1)[None, :]
            valid = pos >= 0
            idx = jnp.maximum(pos, 0)
            kk = kg_all[g][:, idx]
            vv = vg_all[g][:, idx]
            s = jnp.einsum('bqhd,bqkhd->bhqk', qg, kk).astype(jnp.float32) * scale
            p, lse = _masked_softmax(s, valid)
            outs.append(jnp.einsum('bhqk,bqkhd->bqhd', p.astype(vv.dtype), vv))
            lses.append(lse[..., 0])
        wts = jax.nn.softmax(jnp.stack(lses, axis=0), axis=0)
        wts = wts.transpose(0, 1, 3, 2)[..., None].astype(q.dtype)
        return jnp.sum(wts * jnp.stack(outs, axis=0), axis=0)

    out = lax.map(block, jnp.arange(S // Q_BLOCK))
    return out.transpose(1, 0, 2, 3, 4).reshape(B, S, DIL_OUT_W)

def _forgetting_attention(q, k, v, f_logit, f_bias):
    B, S = q.shape[0], q.shape[1]
    scale = HEAD_DIM ** -0.5
    log_f = jax.nn.log_sigmoid(f_logit.astype(jnp.float32) + f_bias.astype(jnp.float32))
    cum = jnp.cumsum(log_f, axis=1)
    cum_k = cum.transpose(0, 2, 1)[:, :, None, :]
    kpos = jnp.arange(S)

    def block(qb):
        q0 = qb * Q_BLOCK
        t = q0 + jnp.arange(Q_BLOCK)
        qblk = lax.dynamic_slice_in_dim(q, q0, Q_BLOCK, axis=1)
        cq = lax.dynamic_slice_in_dim(cum, q0, Q_BLOCK, axis=1).transpose(0, 2, 1)[..., None]
        s = jnp.einsum('bqhd,bkhd->bhqk', qblk, k).astype(jnp.float32) * scale + (cq - cum_k)
        p, _ = _masked_softmax(s, kpos[None, :] <= t[:, None])
        return jnp.einsum('bhqk,bkhd->bqhd', p.astype(v.dtype), v)

    out = lax.map(block, jnp.arange(S // Q_BLOCK))
    return out.transpose(1, 0, 2, 3, 4).reshape(B, S, FOX_W)

def _token_mixing(n, w_in, cmp_pe, cmp_w1, cmp_w2, fox_bias, br_nsa, br_dil, br_fox, w_out, cos, sin):
    B, S = n.shape[0], n.shape[1]
    proj = n @ w_in
    nsa_q, nsa_kv, nsa_g, dil_qkv, fox_qkv, fox_f, merge_g = _split_cols(proj, IN_WIDTHS)

    def heads(t, h):
        return t.reshape(B, S, h, HEAD_DIM)

    def rope_single(t):
        return _partial_rope(t[:, :, None, :], cos, sin)[:, :, 0, :]

    q_a = _partial_rope(heads(nsa_q, NSA_HEADS), cos, sin)
    kc, vc, ks, vs, kw, vw = jnp.split(nsa_kv, 6, axis=-1)
    y_a = _nsa_attention(q_a, rope_single(kc), vc, rope_single(ks), vs, rope_single(kw), vw,
                         nsa_g.reshape(B, S, NSA_HEADS, 3), cmp_pe, cmp_w1, cmp_w2)
    dq, dk, dv = jnp.split(dil_qkv, 3, axis=-1)
    y_b = _dilated_attention(_partial_rope(heads(dq, DIL_HEADS), cos, sin),
                             _partial_rope(heads(dk, DIL_HEADS), cos, sin),
                             heads(dv, DIL_HEADS))
    fq, fk, fv = jnp.split(fox_qkv, 3, axis=-1)
    y_c = _forgetting_attention(heads(fq, FOX_HEADS), heads(fk, FOX_HEADS), heads(fv, FOX_HEADS),
                                fox_f, fox_bias)
    g_a, g_b, g_c = jnp.split(jax.nn.sigmoid(merge_g), 3, axis=-1)
    merged = g_a * (y_a @ br_nsa) + g_b * (y_b @ br_dil) + g_c * (y_c @ br_fox)
    return merged @ w_out

def second_inputs(seed: int = 0) -> dict:
    key = jax.random.key(seed)
    ks = jax.random.split(key, 17)
    L, D = DEPTH, D_MODEL

    def nrm(k, shape, scale):
        return jax.random.normal(k, shape, jnp.float32) * scale

    return {
        'x': nrm(ks[0], (BATCH, SEQ, D), 1.0),
        'c': nrm(ks[1], (BATCH, D), 1.0),
        'ada_w': nrm(ks[2], (L, D, 9 * D), 0.5 * D ** -0.5),
        'ada_b': nrm(ks[3], (L, 9 * D), 0.02),
        'norm_g': 1.0 + nrm(ks[4], (L, 3, D), 0.05),
        'final_norm_g': 1.0 + nrm(ks[5], (D,), 0.05),
        'ffn_w_in': nrm(ks[6], (L, 2, D, 2 * D_FF_2), D ** -0.5),
        'ffn_w_out': nrm(ks[7], (L, 2, D_FF_2, D), D_FF_2 ** -0.5),
        'mix_w_in': nrm(ks[8], (L, D, IN_COLS), D ** -0.5),
        'nsa_cmp_pe': nrm(ks[9], (L, 2, NSA_CMP_LEN, HEAD_DIM), 0.1),
        'nsa_cmp_w1': nrm(ks[10], (L, 2, NSA_CMP_LEN * HEAD_DIM, NSA_CMP_HIDDEN), (NSA_CMP_LEN * HEAD_DIM) ** -0.5),
        'nsa_cmp_w2': nrm(ks[11], (L, 2, NSA_CMP_HIDDEN, HEAD_DIM), NSA_CMP_HIDDEN ** -0.5),
        'fox_f_bias': jax.random.uniform(ks[12], (L, FOX_HEADS), jnp.float32, 1.0, 6.0),
        'br_w_nsa': nrm(ks[13], (L, NSA_Q_W, D), NSA_Q_W ** -0.5),
        'br_w_dil': nrm(ks[14], (L, DIL_OUT_W, D), DIL_OUT_W ** -0.5),
        'br_w_fox': nrm(ks[15], (L, FOX_W, D), FOX_W ** -0.5),
        'mix_w_out': nrm(ks[16], (L, D, D), D ** -0.5),
    }

def second_block(x, c, ada_w, ada_b, norm_g, final_norm_g, ffn_w_in, ffn_w_out, mix_w_in,
              nsa_cmp_pe, nsa_cmp_w1, nsa_cmp_w2, fox_f_bias, br_w_nsa, br_w_dil, br_w_fox,
              mix_w_out):
    S = x.shape[1]
    cos, sin = _rope_tables(S)
    cond = jax.nn.silu(c)
    h = x
    for l in range(DEPTH):
        mod = cond @ ada_w[l] + ada_b[l]
        sh1, sc1, ga1, sh2, sc2, ga2, sh3, sc3, ga3 = [m[:, None, :] for m in jnp.split(mod, 9, axis=-1)]
        n = _modulate(_rms_norm(h, norm_g[l, 0]), sh1, sc1)
        h = h + 0.5 * ga1 * _swiglu(n, ffn_w_in[l, 0], ffn_w_out[l, 0])
        n = _modulate(_rms_norm(h, norm_g[l, 1]), sh2, sc2)
        h = h + ga2 * _token_mixing(n, mix_w_in[l], nsa_cmp_pe[l], nsa_cmp_w1[l], nsa_cmp_w2[l],
                                    fox_f_bias[l], br_w_nsa[l], br_w_dil[l], br_w_fox[l],
                                    mix_w_out[l], cos, sin)
        n = _modulate(_rms_norm(h, norm_g[l, 2]), sh3, sc3)
        h = h + 0.5 * ga3 * _swiglu(n, ffn_w_in[l, 1], ffn_w_out[l, 1])
    return _rms_norm(h, final_norm_g)


def setup_inputs(seed=0):
    out = dict(first_inputs(seed))
    for name, value in second_inputs(seed + 1).items():
        if name != "x":
            out[name + "_2"] = value
    return out


def reference(
    x, positions, ffn1_norm, ffn1_wg, ffn1_wu, ffn1_wd, mix_norm, w_in, conv_w, conv_b,
    conv_ln_g, conv_ln_b, w_out, ffn2_norm, ffn2_wg, ffn2_wu, ffn2_wd, final_norm, c_2, ada_w_2,
    ada_b_2, norm_g_2, final_norm_g_2, ffn_w_in_2, ffn_w_out_2, mix_w_in_2, nsa_cmp_pe_2,
    nsa_cmp_w1_2, nsa_cmp_w2_2, fox_f_bias_2, br_w_nsa_2, br_w_dil_2, br_w_fox_2, mix_w_out_2,
):
    x = first_block(
        x, positions, ffn1_norm, ffn1_wg, ffn1_wu, ffn1_wd, mix_norm, w_in, conv_w, conv_b,
        conv_ln_g, conv_ln_b, w_out, ffn2_norm, ffn2_wg, ffn2_wu, ffn2_wd, final_norm,
    )
    return second_block(
        x, c_2, ada_w_2, ada_b_2, norm_g_2, final_norm_g_2, ffn_w_in_2, ffn_w_out_2, mix_w_in_2,
        nsa_cmp_pe_2, nsa_cmp_w1_2, nsa_cmp_w2_2, fox_f_bias_2, br_w_nsa_2, br_w_dil_2,
        br_w_fox_2, mix_w_out_2,
    )


_drawn_inputs = setup_inputs


def setup_inputs(seed=0):
    import zlib

    import numpy as np

    out = dict(_drawn_inputs(seed))
    spreads = {}
    factors = {'ffn1_norm': 3.795,
     'conv_b': 2.842,
     'conv_ln_g': 5.642,
     'conv_ln_b': 6.081,
     'ffn2_norm': 5.314,
     'final_norm': 2.775,
     'norm_g_2': 3.057,
     'nsa_cmp_pe_2': 7.726}
    for name, (base, spread) in spreads.items():
        noise = np.random.default_rng([zlib.crc32(name.encode()), seed]).standard_normal(out[name].shape)
        drawn = base * np.exp(spread * noise) if base else spread * noise
        out[name] = jnp.asarray(drawn.astype(out[name].dtype))
    for name, factor in factors.items():
        out[name] = (out[name] * factor).astype(out[name].dtype)
    return out
```

```python
import concourse.bass as bass
from concourse import mybir
import numpy as np
from contextlib import ExitStack

F32 = mybir.dt.float32
F32R = mybir.dt.float32r
I32 = mybir.dt.int32
ALU = mybir.AluOpType
ACT = mybir.ActivationFunctionType
AX = mybir.AxisListType

P = 128
D = 1024
FF = 2816
S = 256
NEG = -1e30
EPS = 1e-6

CONST_PARTS = [("ident", 128), ("ones", 128), ("masks", 3 * 256), ("causal", 256), ("decay", 6 * 256),
               ("tri", 256), ("cos2", 16), ("sin2", 16), ("inv", 40), ("cmpm", 30), ("cmp01", 30), ("phalf", 2)]


def const_cols():
    at, out = 0, {}
    for name, n in CONST_PARTS:
        out[name] = (at, n)
        at += n
    return out, at


def constants():
    cols, n = const_cols()
    c = np.zeros((P, n), np.float32)

    def put(name, a):
        o, w = cols[name]
        c[:, o:o + w] = np.asarray(a, np.float32).reshape(P, w)

    i = np.arange(P)[:, None]
    j = np.arange(P)[None, :]
    put("ident", np.eye(P))
    put("ones", np.ones((P, P)))
    m = np.zeros((P, 3, 2, P))
    for g, dil in enumerate((1, 4, 16)):
        off = (j >= i) if g == 0 else ((i - j) % dil == 0)
        m[:, g, 0] = np.where(off, 0.0, NEG)
        m[:, g, 1] = np.where((j <= i) & ((i - j) % dil == 0), 0.0, NEG)
    put("masks", m)
    cm = np.zeros((P, 2, P))
    cm[:, 1] = np.where(j <= i, 0.0, NEG)
    put("causal", cm)
    f = np.float32
    lg = np.log1p(-np.exp2(f(-5.0) - np.arange(6, dtype=np.float32))).astype(np.float32)
    dec = np.zeros((P, 6, 2 * P), np.float32)
    rel = np.arange(2 * P, dtype=np.float32)[None, :] - np.arange(P, dtype=np.float32)[:, None]
    for h in range(6):
        dec[:, h] = np.where(rel >= 0, np.exp(lg[h] * np.maximum(rel, f(0))), 0.0) * f(0.125)
    put("decay", dec)
    t = np.ones((P, 2, P))
    t[:, 0] = i <= j
    put("tri", t)
    inv2 = (f(500000.0) ** (-np.arange(0, 16, 2, dtype=np.float32) / f(16))).astype(np.float32)
    pos = np.arange(2, dtype=np.float32)[None, :, None] * f(128) + np.arange(P, dtype=np.float32)[:, None, None]
    ang = (pos * inv2).astype(np.float32)
    put("cos2", np.cos(ang))
    put("sin2", np.sin(ang))
    ret = (f(10000.0) ** (-np.linspace(0.0, 1.0, 32, dtype=np.float32))).astype(np.float32)
    rope = (f(500000.0) ** (-np.arange(8, dtype=np.float32) / f(8))).astype(np.float32)
    put("inv", np.broadcast_to(np.concatenate([ret, rope]), (P, 40)))
    ends = np.arange(15) * 16 + 31
    ok = ends[None, None, :] <= (np.arange(2)[None, :, None] * 128 + np.arange(P)[:, None, None])
    put("cmpm", np.where(ok, 0.0, NEG))
    put("cmp01", ok)
    c[:, cols["phalf"][0]] = -0.5
    c[:, cols["phalf"][0] + 1] = np.pi / 2
    return c


class Line:

    def __init__(self, sem):
        self.sem, self.n, self.items = sem, 0, []

    def put(self, fn, waits, inc=True):
        self.items.append((fn, [w for w in waits if w is not None], inc))
        if inc:
            self.n += 1
            return (self.sem, self.n)
        return None

    def put_dma(self, fn, waits, sem):
        self.items.append((fn, [w for w in waits if w is not None], sem))

    def play(self, eng):
        seen = {}
        for fn, waits, inc in self.items:
            for sem, v in waits:
                if seen.get(id(sem), 0) < v:
                    eng.wait_ge(sem, v)
                    seen[id(sem)] = v
            if fn is None:
                continue
            ins = fn(eng)
            if inc is True:
                ins.then_inc(self.sem, 1)
            elif inc is not False:
                ins.then_inc(inc, 16)


NR = 4
NH = 5
LA = 3


def program(nc, A, out, dbg=None, stop=99):
    ctx = ExitStack()
    with ctx:
        top = [(nc.sbuf_base + 63) // 64 * 64]

        def place(name, shape, dt, at):
            return nc.alloc_sbuf_tensor_at(name, shape, dt, offset=at)

        def size(shape):
            n = 4
            for s in shape[1:]:
                n *= s
            return (n + 31) // 32 * 32

        def sb(name, shape, dt=F32):
            t = place(name, shape, dt, top[0])
            top[0] += size(shape)
            return t

        def sem(name):
            return ctx.enter_context(nc.semaphore(name))

        cols, NC = const_cols()
        cst = sb("cst", [P, NC])

        def C(name):
            o, w = cols[name]
            return cst[:, o:o + w]

        ident = C("ident")
        ones = C("ones")
        masks = C("masks").rearrange("p (g b k) -> p g b k", g=3, b=2)
        causal = C("causal")
        decay = C("decay").rearrange("p (h c) -> p h c", h=6)
        tri = C("tri")
        phalf = C("phalf")
        cos2 = C("cos2").rearrange("p (t f) -> p t f", t=2)
        sin2 = C("sin2").rearrange("p (t f) -> p t f", t=2)

        x = sb("x", [P, 2, D])
        xh = sb("xh", [P, 8, S], F32R)
        xl = sb("xl", [P, 8, S], F32R)
        raw = [sb(f"raw{i}", [P, 2048]) for i in range(NR)]
        wh = [sb(f"wh{i}", [P, 1024], F32R) for i in range(NH)]
        wl = [sb(f"wl{i}", [P, 1024], F32R) for i in range(NH)]
        cols1 = sb("cols1", [P, 104])
        cols2 = sb("cols2", [P, 128])
        cols3 = sb("cols3", [P, 64])
        condT = sb("condT", [P, 8])
        w2d = sb("w2d", [P, 2, 3, 64])
        cos1 = sb("cos1", [P, 2, 40])
        sin1 = sb("sin1", [P, 2, 40])
        gaB = [sb(f"gaB{i}", [P, D]) for i in range(2)]
        lngb = place("lngb", [P, 2, 2, 256], F32, top[0])
        acc = [sb(f"acc{i}", [P, 512]) for i in range(2)]
        bt = [sb(f"bt{i}", [P, 512]) for i in range(2)]
        shc = [sb(f"shc{i}", [P, 8]) for i in range(2)]
        Gc = [sb(f"Gc{i}", [P, 8]) for i in range(2)]
        ssq = sb("ssq", [P, 4])
        ms = sb("ms", [P, 4])
        rr = sb("rr", [P, 2])
        U0 = top[0]
        END = [U0]

        def region(start):
            cur = [start]

            def put(name, shape, dt=F32):
                t = place(name, shape, dt, cur[0])
                cur[0] += size(shape)
                END[0] = max(END[0], cur[0])
                return t
            return put, cur

        fz, fcur = region(U0)
        hTh = fz("hTh", [P, 22, S], F32R)
        hTl = fz("hTl", [P, 22, S], F32R)
        sg = [fz(f"sg{i}", [P, 512]) for i in range(2)]
        hb = [[fz(f"hb{i}{t}", [P, 512]) for t in range(2)] for i in range(2)]
        nz, _ = region(fcur[0])
        xn = nz("xn", [P, 2, D])
        vT = xn[:, :, :].rearrange("p t n -> p (t n)").rearrange("p (k s) -> p k s", s=S)
        mz, mcur = region(U0)
        zt = [mz(f"zt{i}", [P, 2, 512]) for i in range(2)]
        dup = place("dup", [P, 2, 4, 128], F32, mcur[0])
        pt_ = [mz(f"pt{i}", [P, 768]) for i in range(2)]
        rt = [place(f"rt{i}", [P, 2, 192], F32, mcur[0] + 1536 * i) for i in range(4)]
        ptT = [mz(f"ptT{i}", [P, 768]) for i in range(2)]
        ym = mz("ym", [P, 2, D])
        small = mz("small", [P, 256])
        m0 = mcur[0]
        m1, _ = region(m0)
        v1 = [m1("rv", [P, 2, 384]), m1("mv", [P, 2, 384])]
        rg = m1("rg", [P, 2, 384])
        qk1 = {n: m1("T" + n, [P, 3, S]) for n in ("rq", "rk", "mq", "mk")}
        upad = m1("upad", [P, 2, 288])
        cacc = m1("cacc", [P, 2, S])
        yc = m1("yc", [P, 2, 256])
        yc2 = m1("yc2", [P, 2, 256])
        m2, _ = region(m0)
        gts = m2("gts", [P, 2, 3, D])
        qk2 = {n: m2("T" + n, [P, 3, S]) for n in ("dq", "dk", "fq", "fk")}
        qn = m2("qn", [P, 2, S])
        kd = m2("kd", [P, 4, S])
        vn = m2("vn", [P, 2, 2, 64])
        vd = m2("vd", [P, 2, 384])
        vf = m2("vf", [P, 2, 384])
        ng = m2("ng", [P, 2, 12])
        logf = m2("logf", [P, 2, 6])
        cq = m2("cq", [P, 2, 6])
        assert END[0] <= nc.sbuf_usable_end, (END[0], nc.sbuf_usable_end)

        ps = [ctx.enter_context(nc.psum_tensor(f"ps{i}", [P, 512], F32)) for i in range(4)]
        s45 = ctx.enter_context(nc.psum_tensor("s45", [P, 1024], F32))
        ps += [s45[:, 0:512], s45[:, 512:1024]]
        ps += [ctx.enter_context(nc.psum_tensor(f"ps{i}", [P, 512], F32)) for i in range(6, 8)]
        ps = [p[:, :] for p in ps]

        PE, AC, DV, PO, SP = (Line(sem(n)) for n in ("s_pe", "s_act", "s_dve", "s_pool", "s_sp"))
        s_raw = [sem(f"s_raw{i}") for i in range(NR)]
        n_raw = [0] * NR
        s_bt = [sem(f"s_bt{i}") for i in range(2)]
        n_bt = [0] * 2
        s_cst = sem("s_cst")
        s_rows = sem("s_rows")
        s_x = sem("s_x")
        s_misc = sem("s_misc")
        s_fin = [sem("s_fin0"), sem("s_fin1")]
        s_out = sem("s_out")

        def mm(o, l, r, start, stop, w=(), inc=False):
            return PE.put(lambda e: e.matmul(o, l, r, start=start, stop=stop), w, inc)

        def tr(o, i, w=(), inc=False):
            n = i.shape[0]
            return PE.put(lambda e: e.transpose(o, i, ident[0:n, 0:n]), w, inc)

        def act(o, i, f, w=(), **kw):
            return AC.put(lambda e: e.activation(o, i, f, **kw), w)

        def tt(o, a, b, op, w=(), L=None):
            return (L or DV).put(lambda e: e.tensor_tensor(o, a, b, op), w)

        def ts(o, a, s1, s2, op0, op1=None, w=(), L=None):
            if op1 is None:
                return (L or DV).put(lambda e: e.tensor_scalar(o, a, s1, None, op0), w)
            return (L or DV).put(lambda e: e.tensor_scalar(o, a, s1, s2, op0, op1), w)

        def stt(o, a, s, b, op0, op1, w=()):
            return DV.put(lambda e: e.scalar_tensor_tensor(out=o, in0=a, scalar=s, in1=b, op0=op0, op1=op1), w)

        def cp(o, a, w=(), L=None):
            return (L or DV).put(lambda e: e.tensor_copy(o, a), w)

        def red(o, a, op, w=()):
            return DV.put(lambda e: e.tensor_reduce(o, a, AX.X, op), w)

        def rec(o, a, w=()):
            return DV.put(lambda e: e.reciprocal(o, a), w)

        def ttr(o, a, b, red_, w=()):
            return DV.put(lambda e: e.tensor_tensor_reduce(o, a, b, 1.0, -3e38, ALU.add, ALU.max, red_), w)

        def dma(L, o, i, s, w=()):
            L.put_dma(lambda e: e.dma_start(o, i), w, s)

        units = []

        def wview(W, k0, nk, c0, w):
            return W[k0 * P:(k0 + nk) * P, c0:c0 + w].rearrange("(k p) n -> p k n", p=P)

        def add_gemm(label, W, K, c0, w):
            nk = 4 if w > 256 else 8
            for k0 in range(0, K, nk):
                n = min(nk, K - k0)
                units.append(dict(kind="w", label=label, nk=n, w=w, per=2 if w > 256 else 4,
                                  src=[(wview(W, k0, n, c0, w), 0, w)]))

        def add_ada(n):
            for _ in range(n):
                if ada_at[0] < 72:
                    q, half = divmod(ada_at[0], 2)
                    s_, i = divmod(q, 6)
                    l, j = divmod(s_, 3)
                    W = A["ada_w_2"][l]
                    units.append(dict(kind="a", label=None, nk=4, w=512, q=q, half=half,
                                      src=[(wview(W, 4 * half, 4, (6 * j + i) * 512, 512), 0, 512)]))
                    ada_at[0] += 1

        ada_at = [0]

        def plan_ffn(label, Wg, g0, Wu, u0, Wd, ada):
            n = 0
            for c in range(6):
                if c < 5:
                    add_gemm(label + "g", Wg, 8, g0 + 512 * c, 512)
                    add_gemm(label + "u", Wu, 8, u0 + 512 * c, 512)
                else:
                    for k0 in (0, 4):
                        units.append(dict(kind="w", label=label + "gu", nk=4, w=512, per=2, src=[
                            (wview(Wg, k0, 4, g0 + 2560, 256), 0, 256), (wview(Wu, k0, 4, u0 + 2560, 256), 256, 256)]))
                if ada:
                    add_ada(2 if c < 5 else 0)
            for h in range(2):
                add_gemm(label + "d", Wd, 22, 512 * h, 512)
                if ada and h == 0:
                    add_ada(2)

        L1CH = [("c", 2688, 512), ("mq", 1536, 384), ("mk", 1920, 384), ("mv", 2304, 384),
                ("rq", 0, 384), ("rk", 384, 384), ("rv", 768, 384), ("rg", 1152, 384)]
        L2CH = [("n0", 0, 512), ("n1", 512, 140), ("dq", 652, 384), ("dk", 1036, 384), ("dv", 1420, 384),
                ("fq", 1804, 384), ("fk", 2188, 384), ("fv", 2572, 390)]
        SUBS = ["f1", "m", "f2"] * 2 + ["F1", "M", "F2"] * 2
        for si, kind in enumerate(SUBS[:stop] if stop < 99 else SUBS):
            l = (si // 3) % 2
            if kind in ("f1", "f2"):
                n = "ffn" + kind[1]
                plan_ffn(kind, A[n + "_wg"][l], 0, A[n + "_wu"][l], 0, A[n + "_wd"][l], si == 5)
            elif kind == "m":
                for n, c0, w in L1CH:
                    add_gemm(n, A["w_in"][l], 8, c0, w)
                for h in range(2):
                    add_gemm("wo", A["w_out"][l], 8, 512 * h, 512)
            elif kind in ("F1", "F2"):
                b = int(kind[1]) - 1
                W = A["ffn_w_in_2"][l, b]
                plan_ffn(kind, W, 0, W, FF, A["ffn_w_out_2"][l, b], True)
            else:
                W = A["mix_w_in_2"][l]
                for i, (n, c0, w) in enumerate(L2CH):
                    add_gemm(n, W, 8, c0, w)
                    add_ada(2 if i >= 2 else 0)
                for kv in range(2):
                    units.append(dict(kind="r", label="w1", nk=16, w=128, src=[
                        (A["nsa_cmp_w1_2"][l, kv].rearrange("(j p) n -> p j n", p=P), 0, 128)]))
                for b in range(6):
                    add_gemm("mg", W, 8, 2962 + 512 * b, 512)
                for h in range(2):
                    units.append(dict(kind="w", label="br", nk=3, w=512, per=2, src=[
                        (wview(A["br_w_nsa_2"][l], 0, 2, 512 * h, 512), 0, 512, 0, 2),
                        (wview(A["br_w_dil_2"][l], 0, 1, 512 * h, 512), 0, 512, 2, 3)]))
                    add_gemm("br", A["br_w_fox_2"][l], 3, 512 * h, 512)
                for h in range(2):
                    add_gemm("wo2", A["mix_w_out_2"][l], 8, 512 * h, 512)

        subs = []
        for u, un in enumerate(units):
            if un["kind"] == "w":
                for k0 in range(0, un["nk"], un["per"]):
                    subs.append((u, k0, min(un["per"], un["nk"] - k0)))
            else:
                subs.append((u, 0, un["nk"]))

        issued = [0]
        raw_tok = {}
        raw_done = {}

        def issue(u):
            if u >= len(units):
                return
            assert u == issued[0]
            issued[0] += 1
            un, slot = units[u], u % NR
            view = raw[slot][:, 0:un["nk"] * un["w"]].rearrange("p (k n) -> p k n", n=un["w"])
            for piece in un["src"]:
                src, c0, w = piece[:3]
                k0, k1 = piece[3:] if len(piece) > 3 else (0, un["nk"])
                dma(SP, view[:, k0:k1, c0:c0 + w], src, s_raw[slot], raw_done.get(u - NR, ()))
                n_raw[slot] += 16
            raw_tok[u] = (s_raw[slot], n_raw[slot])

        bfree = [[] for _ in range(8)]
        made = [0]
        wsub = [0]
        ready = {}
        hfree = {}
        cond_tok = [None]
        bt_ready = [None] * 2
        bt_all = []
        accr = [[], []]
        reduces = []
        reduced = [-1]
        gab_free = [[], []]
        col_free = [[], []]
        ada_tok = {}
        macs = {}

        def bt_issue(q, w):
            if q >= 36:
                return
            s_, i = divmod(q, 6)
            l, j = divmod(s_, 3)
            o = (6 * j + i) * 512
            dma(SP, bt[q % 2][0:1, :], A["ada_b_2"][l:l + 1, o:o + 512], s_bt[q % 2], w)
            n_bt[q % 2] += 16
            bt_ready[q % 2] = (s_bt[q % 2], n_bt[q % 2])
            bt_all.append(bt_ready[q % 2])

        def make():
            u, k0, nk = subs[made[0]]
            un, slot = units[u], u % NR
            made[0] += 1
            last = made[0] == len(subs) or subs[made[0]][0] != u
            if un["kind"] == "w":
                j = wsub[0]
                wsub[0] += 1
                hs = j % NH
                n = nk * un["w"]
                src = raw[slot][:, k0 * un["w"]:k0 * un["w"] + n]
                hi, lo = wh[hs][:, 0:n], wl[hs][:, 0:n]
                free = hfree.get(j - NH)
                th = act(hi, src, ACT.Copy, [raw_tok[u], free])
                tl = tt(lo, src, hi.bitcast(F32), ALU.subtract, [raw_tok[u], th, free])
                ready[j] = (hs, nk, un, tl)
                if last:
                    raw_done[u] = [tl]
                    issue(u + NR)
            elif un["kind"] == "r":
                j = wsub[0]
                wsub[0] += 1
                ready[j] = (u, nk, un, raw_tok[u])
            else:
                q = un["q"]
                a = acc[q % 2]
                for k in range(4):
                    kk = 4 * un["half"] + k
                    wl_ = [raw_tok[u], cond_tok[0]]
                    if kk == 0:
                        assert reduced[0] >= q - 2
                        prev = bt[q % 2][:, :]
                        wl_ += [bt_ready[q % 2]] + accr[q % 2]
                    else:
                        prev = a[:, :]
                        wl_ += [macs[q]]
                    t = stt(a[:, :], raw[slot][:, k * 512:k * 512 + 512], condT[:, kk:kk + 1], prev,
                            ALU.mult, ALU.add, wl_)
                    macs[q] = t
                    if kk == 0:
                        bt_issue(q + 2, [t])
                raw_done[u] = [t]
                issue(u + NR)
                if un["half"]:
                    reduces.append((q, t))

        def free_raw(u, tok):
            raw_done[u] = [tok]
            issue(u + NR)

        taken = [0]

        def take(label):
            j = taken[0]
            taken[0] += 1
            while wsub[0] <= j:
                make()
            hs, nk, un, tok = ready.pop(j)
            assert un["label"] == label, (un["label"], label)
            return j, hs, nk, un, tok

        def ahead():
            while wsub[0] < taken[0] + LA and made[0] < len(subs):
                if units[subs[made[0]][0]]["kind"] == "r":
                    break
                make()

        def flush():
            while reduces:
                q, tok = reduces.pop(0)
                reduce_mod(q, tok)
                reduced[0] = q

        tbank = [6]

        def next_t():
            tbank[0] = 13 - tbank[0]
            return tbank[0]

        def reduce_mod(q, tok):
            s_, i = divmod(q, 6)
            a, b = acc[q % 2], next_t()
            if i < 4:
                for k in range(4):
                    t = mm(ps[b][:, k:k + 1], a[:, k * P:(k + 1) * P], ones[:, 0:1], True, True,
                           [tok] + bfree[b], inc=(k == 3))
                o = 4 * (i % 2)
                if i < 2:
                    r = cp(shc[s_ % 2][:, o:o + 4], ps[b][:, 0:4], [t] + col_free[s_ % 2])
                else:
                    g = cols1[:, 48 + 8 * s_ + o:48 + 8 * s_ + o + 4]
                    r = stt(Gc[s_ % 2][:, o:o + 4], ps[b][:, 0:4], 1.0, g, ALU.add, ALU.mult, [t] + col_free[s_ % 2])
                bfree[b] = [r]
            else:
                t = mm(ps[b], ones, a[:, :], True, True, [tok] + bfree[b], inc=True)
                o = 512 * (i - 4)
                r = act(gaB[s_ % 2][:, o:o + 512], ps[b], ACT.Copy, [t] + gab_free[s_ % 2],
                        scale=1.0 if s_ % 3 == 1 else 0.5)
                bfree[b] = [r]
            accr[q % 2] = [t]
            ada_tok.setdefault(s_, []).append(r)

        def gemm_sub(label, banks, hiT, loT, kpos, K, xw):
            j, hs, nk, un, tok = take(label)
            w = un["w"]
            for k in range(nk):
                kk = kpos + k
                hi, lo = wh[hs][:, k * w:(k + 1) * w], wl[hs][:, k * w:(k + 1) * w]
                for t in range(2):
                    b = banks[t]
                    o = ps[b][:, 0:w]
                    a, c = hiT(kk, t), loT(kk, t)
                    ww = [tok] + xw(kk)
                    if kk == 0:
                        ww += bfree[b]
                    end = kk == K - 1
                    mm(o, a, hi, kk == 0, False, ww)
                    mm(o, a, lo, False, False)
                    t_ = mm(o, c, hi, False, end, inc=(k == nk - 1 and t == 1))
            hfree[j] = t_
            ahead()
            return nk, t_

        def gemm(label, banks, hiT, loT, K, xw):
            k = 0
            while k < K:
                n, t = gemm_sub(label, banks, hiT, loT, k, K, xw)
                k += n
            return t

        XH = lambda k, t: xh[:, k, t * P:(t + 1) * P]
        XL = lambda k, t: xl[:, k, t * P:(t + 1) * P]
        x_ready = {}

        def XW(k):
            return x_ready[k // 2]

        rows = U0
        rows1 = place("rows1", [P, 128], F32, rows)
        rows2 = place("rows2", [P, 128], F32, rows + 512)
        rows3 = place("rows3", [P, 128], F32, rows + 1024)
        posi = place("posi", [P, 128], I32, rows + 1536)
        posr = place("posr", [P, 128], F32, rows + 2048)
        posf = place("posf", [P, 2], F32, rows + 2560)
        an = [place(f"an{i}", [P, 2, 40], F32, rows + 2592 + 320 * i) for i in range(3)]

        dma(AC, cst[:, :], A["cst"], s_cst)
        nrow = 0
        o = 0
        for n, k in (("ffn1_norm", 16), ("mix_norm", 16), ("ffn2_norm", 16)):
            dma(AC, rows1[o:o + k, :], A[n].rearrange("l (k p) -> (l k) p", p=P), s_rows)
            o += k
        dma(AC, rows1[48:96, :], A["norm_g_2"].rearrange("l s (k p) -> (l s k) p", p=P), s_rows)
        dma(AC, rows1[96:104, :], A["c_2"].rearrange("a (k p) -> (a k) p", p=P), s_rows)
        nrow = 5
        for l in range(2):
            for c in range(2):
                o = (2 * l + c) * 31
                dma(AC, rows2[o:o + 31, :], A["conv_w"][l, :, c * P:(c + 1) * P], s_rows)
                nrow += 1
        dma(AC, rows2[124:128, :], A["conv_b"].rearrange("l (c p) -> (l c) p", p=P), s_rows)
        dma(AC, rows3[0:64, :], A["nsa_cmp_pe_2"].rearrange("l v (j b) d -> (l v j) (b d)", b=2), s_rows)
        dma(AC, posi[0:2, :], A["positions"].rearrange("a (t p) -> (a t) p", p=P), s_rows)
        nrow += 3
        n_misc = 0
        for l in range(2):
            for a, b in ((0, 0), (0, 1), (1, 2)):
                dma(AC, w2d[:, l, b, :], A["nsa_cmp_w2_2"][l, a], s_misc)
                n_misc += 16
            dma(AC, lngb[:, l, 0, :], A["conv_ln_g"][l].partition_broadcast(P), s_misc)
            dma(AC, lngb[:, l, 1, :], A["conv_ln_b"][l].partition_broadcast(P), s_misc)
            n_misc += 32
        CST, ROWS, MISC = (s_cst, 16), (s_rows, 16 * nrow), (s_misc, n_misc)
        for t in range(2):
            dma(SP, x[:, t, :], A["x"][0, t * P:(t + 1) * P, :], s_x)
        X0 = (s_x, 32)

        tz = [DV.put(lambda e, i=i: e.memset(bt[i][:, :], 0.0), []) for i in range(2)]
        for u in range(NR):
            issue(u)
        bt_issue(0, [tz[0]])
        bt_issue(1, [tz[1]])

        t = tr(ps[6][:, 0:104], rows1[0:104, :], [CST, ROWS], inc=True)
        g1 = cp(cols1[:, :], ps[6][:, 0:104], [t])
        t = tr(ps[7][:, 0:128], rows2[:, :], inc=True)
        g2 = cp(cols2[:, :], ps[7][:, 0:128], [t])
        t = tr(ps[5][:, 0:64], rows3[0:64, :], inc=True)
        g3 = cp(cols3[:, :], ps[5][:, 0:64], [t])
        bfree[6] = [g1]
        bfree[5] = [g3]
        bfree[7] = [g2]
        COLS = g3
        cond_tok[0] = act(condT[:, :], cols1[:, 96:104], ACT.Silu, [g1])
        inv = C("inv")
        t = cp(posr[0:2, :], posi[0:2, :], [ROWS])
        t = tr(ps[4][:, 0:2], posr[0:2, :], [t], inc=True)
        t = cp(posf[:, :], ps[4][:, 0:2], [t])
        bfree[4] = [t]
        for i in range(2):
            ta = ts(an[0][:, i, :], inv, posf[:, i:i + 1], None, ALU.mult, w=[t, CST])
        MAGIC = 12582912.0
        tb_ = ts(an[1][:, :, :], an[0][:, :, :], float(np.float32(1 / (2 * np.pi))), MAGIC, ALU.mult, ALU.add, w=[ta])
        tb_ = ts(an[1][:, :, :], an[1][:, :, :], -MAGIC, None, ALU.add, w=[tb_])
        c1 = 6.28125
        c2 = float(np.float32(round((2 * np.pi - c1) * 2 ** 21) / 2 ** 21))
        c3 = float(np.float32(2 * np.pi - c1 - c2))
        for cc in (c1, c2, c3):
            tb_ = stt(an[0][:, :, :], an[1][:, :, :], -cc, an[0][:, :, :], ALU.mult, ALU.add, [tb_])
        pi_ = float(np.nextafter(np.float32(np.pi), np.float32(0)))
        tb_ = ts(an[0][:, :, :], an[0][:, :, :], pi_, -pi_, ALU.min, ALU.max, w=[tb_])
        tc_ = stt(an[2][:, :, :], an[0][:, :, :], -1.0, an[0][:, :, :], ALU.mult, ALU.max, [tb_])
        act(sin1[:, :, :], an[0][:, :, :], ACT.Sin, [tb_])
        TRIG = act(cos1[:, :, :], an[2][:, :, :], ACT.Sin, [tc_, CST], scale=-1.0, bias=phalf[:, 1:2])
        last_pe = [None]

        xr = {(t, h): [X0] for t in range(2) for h in range(2)}
        junk = [None]

        def row_scale():
            tk = []
            for h in range(2):
                for t in range(2):
                    tk.append(act(xn[:, t, h * 512:(h + 1) * 512], x[:, t, h * 512:(h + 1) * 512], ACT.Square,
                                  xr[t, h] + [TRIG], accum_out=ssq[:, 2 * h + t:2 * h + t + 1]))
            a = tt(ms[:, 0:2], ssq[:, 0:2], ssq[:, 2:4], ALU.add, tk)
            a = ts(ms[:, 2:4], ms[:, 0:2], 1.0 / D, EPS, ALU.mult, ALU.add, w=[a])
            return tt(rr[:, :], ms[:, 2:4], phalf[:, 0:1].broadcast_to([P, 2]), ALU.pow, [a, CST], L=PO), tk[-1]

        def split_x(b, k, tok, xw):
            hi = xh[:, k:k + 2, :].rearrange("p k s -> p (k s)")
            lo = xl[:, k:k + 2, :].rearrange("p k s -> p (k s)")
            th = act(hi, ps[b], ACT.Copy, [tok] + xw)
            tl = tt(lo, ps[b], hi.bitcast(F32), ALU.subtract, [th])
            bfree[b] = [tl]
            x_ready[k // 2] = [tl]

        def turn_x(src, w, nk=8, banks=(4, 5, 6, 7)):
            done = []
            for k in range(0, nk, 2):
                b = banks[k // 2 % len(banks)]
                for kk in range(2):
                    for t in range(2):
                        tk = tr(ps[b][:, kk * 256 + t * P:kk * 256 + (t + 1) * P], src(k + kk, t),
                                w + bfree[b], inc=(kk == 1 and t == 1))
                done.append((b, k, tk))
            return done

        def norm_x(gcol, scol, gw):
            r, sq = row_scale()
            w = []
            w.append(ts(xn[:, 0, :], x[:, 0, :], rr[:, 0:1], None, ALU.mult, w=[r, sq]))
            w.append(act(xn[:, 1, :], x[:, 1, :], ACT.Copy, [r, sq], scale=rr[:, 1:2]))
            last = last_pe[0]
            done = turn_x(lambda k, t: xn[:, t, k * P:(k + 1) * P], w)
            for b, k, tk in done:
                fin = done[-1][2]
                for kk in range(2):
                    s1 = gcol(k + kk)
                    o = vT[:, k + kk, :]
                    i = ps[b][:, kk * 256:(kk + 1) * 256]
                    if scol is None:
                        tv = ts(o, i, s1, None, ALU.mult, w=[tk, fin] + gw)
                    else:
                        tv = ts(o, i, s1, scol(k + kk), ALU.mult, ALU.add, w=[tk, fin] + gw)
                bfree[b] = [tv]
                hi, lo = xh[:, k:k + 2, :], xl[:, k:k + 2, :]
                th = act(hi, vT[:, k:k + 2, :], ACT.Copy, [tv, last])
                tl = tt(lo, vT[:, k:k + 2, :], hi.bitcast(F32), ALU.subtract, [th, last])
                x_ready[k // 2] = [tl]
            return tv

        def add_x(t, h, b, tok, ga):
            xs = x[:, t, h * 512:(h + 1) * 512]
            if ga is None:
                r = stt(xs, ps[b], 0.5, xs, ALU.mult, ALU.add, [tok])
            elif ga == 1:
                r = tt(xs, ps[b], xs, ALU.add, [tok])
            else:
                r = tt(ps[b], ps[b], gaB[ga[0] % 2][:, h * 512:(h + 1) * 512], ALU.mult, [tok] + ada_tok[ga[0]])
                r = tt(xs, ps[b], xs, ALU.add, [r])
                gab_free[ga[0] % 2] = [r]
            bfree[b] = [r]
            xr[t, h] = [r]

        sg_free = [None, None]
        hb_ready = {}
        hb_free = {}

        def ffn(label, gcol, scol, gw, ga):
            tv = norm_x(gcol, scol, gw)
            if ga is not None:
                col_free[ga[0] % 2] = [tv]
            ring = [0]

            def banks():
                b = (ring[0] % 6, (ring[0] + 1) % 6)
                ring[0] += 2
                return b

            def turn_h(c):
                nb = 4 if c < 5 else 2
                for i in range(0, nb, 2):
                    b = next_t()
                    for ii in range(2):
                        for t in range(2):
                            tk = tr(ps[b][:, ii * 256 + t * P:ii * 256 + (t + 1) * P],
                                    hb[c % 2][t][:, (i + ii) * P:(i + ii + 1) * P],
                                    hb_ready[c] + bfree[b], inc=(ii == 1 and t == 1))
                    k = 4 * c + i
                    hi = hTh[:, k:k + 2, :].rearrange("p k s -> p (k s)")
                    lo = hTl[:, k:k + 2, :].rearrange("p k s -> p (k s)")
                    th = act(hi, ps[b], ACT.Copy, [tk])
                    tl = tt(lo, ps[b], hi.bitcast(F32), ALU.subtract, [th])
                    bfree[b] = [tl]
                    h_ready[k // 2] = [tl]
                hb_free[c] = [tk]

            h_ready = {}
            for c in range(6):
                if c < 5:
                    bg, bu = banks(), banks()
                    n, _ = gemm_sub(label + "g", bg, XH, XL, 0, 8, XW)
                    k = n
                    while k < 8:
                        n, tg = gemm_sub(label + "g", bg, XH, XL, k, 8, XW)
                        k += n
                    if c:
                        turn_h(c - 1)
                    flush()
                    tu = gemm(label + "u", bu, XH, XL, 8, XW)
                    w = 512
                else:
                    bg = bu = banks()
                    n, _ = gemm_sub(label + "gu", bg, XH, XL, 0, 8, XW)
                    k = n
                    while k < 8:
                        n, tg = gemm_sub(label + "gu", bg, XH, XL, k, 8, XW)
                        k += n
                    tu = tg
                    turn_h(c - 1)
                    flush()
                    w = 256
                rd = []
                for t in range(2):
                    g = ps[bg[t]][:, 0:w]
                    uu = ps[bu[t]][:, 0:w] if c < 5 else ps[bu[t]][:, 256:512]
                    ta = act(sg[t][:, 0:w], g, ACT.Silu, [tg, sg_free[t]])
                    th = tt(hb[c % 2][t][:, 0:w], uu, sg[t][:, 0:w], ALU.mult, [ta, tu] + hb_free.get(c - 2, []))
                    sg_free[t] = th
                    bfree[bg[t]] = [th]
                    bfree[bu[t]] = [th]
                    rd.append(th)
                hb_ready[c] = rd
            last_pe[0] = tu
            HH = lambda k, t: hTh[:, k, t * P:(t + 1) * P]
            HL = lambda k, t: hTl[:, k, t * P:(t + 1) * P]
            for h in range(2):
                b = banks()
                k = 0
                while k < 22:
                    n, td = gemm_sub(label + "d", b, HH, HL, k, 22, lambda kk: h_ready[kk // 2])
                    k += n
                    if h == 0 and k == 4:
                        turn_h(5)
                    if k == 12:
                        flush()
                for t in range(2):
                    add_x(t, h, b[t], td, ga)
            hb_free.clear()

        class Step:
            pass

        sbuf_free = [None, None]
        ptT_free = [None, None]
        nstep = [0]

        def attention(steps, fill):
            prev = None
            for st in steps + [None]:
                if st is not None:
                    scores(st)
                    fill()
                if prev is not None:
                    values(prev)
                    fill()
                prev = st

        def scores(st):
            n = nstep[0]
            nstep[0] += 1
            st.i = n % 2
            if st.wide:
                base, bb = 0, (4, 5)
            else:
                base, bb = 512 * (n % 2), (4 + n % 2,)
            st.tk = []
            P_ = pt_[st.i]
            if st.pre is not None:
                st.pre(st)
            for sgm in st.segs:
                o = sgm["o"]
                for pi, (q, k, w, m) in enumerate(sgm["parts"]):
                    free = [f for b in bb for f in bfree[b]]
                    tk = mm(s45[:, base + o:base + o + w], q, k, True, True, free + st.w, inc=True)
                    o += w
                sgm["w"] = o - sgm["o"]
            rd = []
            for sgm in st.segs:
                o, w, t = sgm["o"], sgm["w"], sgm["t"]
                d = P_[:, o:o + w]
                src = s45[:, base + o:base + o + w]
                mx = st.sm[:, t:t + 1]
                if st.fox is None:
                    m = sgm["mask"]
                    sp = d
                    if len(m.shape) == 3:
                        src = src.rearrange("p (g k) -> p g k", k=m.shape[2])
                        sp = d.rearrange("p (g k) -> p g k", k=m.shape[2])
                    ta = tt(sp, src, m, ALU.add, [tk, sbuf_free[st.i], CST])
                else:
                    ta = stt(d, src, 0.125, st.fox(t), ALU.mult, ALU.subtract, [tk, sbuf_free[st.i]] + st.foxw)
                tm = red(mx, d, ALU.max, [ta])
                rd.append(ta)
                tn = ts(st.sm[:, 2 + t:3 + t], mx, -st.scale, None, ALU.mult, w=[tm])
                te = act(d, d, ACT.Exp, [tn], bias=st.sm[:, 2 + t:3 + t], scale=st.scale,
                         accum_out=st.sm[:, 4 + t:5 + t])
                trc = rec(st.sm[:, 6 + t:7 + t], st.sm[:, 4 + t:5 + t], [te])
                sgm["e"] = te
                sgm["r"] = trc
            for b in bb:
                bfree[b] = list(rd)

        def values(st):
            P_, T_ = pt_[st.i], ptT[st.i]
            blocks = []
            for sgm in st.segs:
                o = sgm["o"]
                for pi, (q, k, w, m) in enumerate(sgm["parts"]):
                    for kb in range(w // P):
                        blocks.append((sgm, o, pi, kb))
                        o += P
            done = {}
            for r0 in range(0, len(blocks), 4):
                grp = blocks[r0:r0 + 4]
                for gi, (sgm, o, pi, kb) in enumerate(grp):
                    tk = tr(ps[6][:, gi * P:(gi + 1) * P], P_[:, o:o + P], [sgm["e"]] + bfree[6], inc=(gi == len(grp) - 1))
                n = len(grp) * P
                tc = act(T_[:, r0 * P:r0 * P + n], ps[6][:, 0:n], ACT.Copy, [tk, ptT_free[st.i]])
                bfree[6] = [tc]
                for gi in range(len(grp)):
                    done[r0 + gi] = tc
            sbuf_free[st.i] = tk
            for sgm in st.segs:
                idx = [i for i, bl in enumerate(blocks) if bl[0] is sgm]
                o = st.i * 128 + sgm["t"] * 64
                for n, i in enumerate(idx):
                    _, _, pi, kb = blocks[i]
                    tk = mm(ps[7][:, o:o + 64], T_[:, i * P:(i + 1) * P], st.v(pi, kb), n == 0, n == len(idx) - 1,
                            [done[i]] + bfree[7] + st.w, inc=(n == len(idx) - 1))
                sgm["o_ps"] = ps[7][:, o:o + 64]
            ptT_free[st.i] = tk
            rd = []
            for sgm in st.segs:
                rd.append(st.out(sgm["t"], sgm["o_ps"], st.sm[:, 6 + sgm["t"]:7 + sgm["t"]], [tk, sgm["r"]]))
            st.done = rd
            o_free[st.i] = rd
            bfree[7] = list(rd)

        o_free = [[], []]

        def pair_step(i, qT, kT, v, mask, outf, w, fox=None, foxw=(), scale=0.125, pre=None):
            st = Step()
            st.wide = False
            st.segs = [dict(t=0, o=0, parts=[(qT[:, 0:P], kT[:, 0:P], P, None)], mask=mask[:, P:2 * P] if mask is not None else None),
                       dict(t=1, o=P, parts=[(qT[:, P:S], kT[:, 0:S], S, None)], mask=mask)]
            st.v, st.out, st.w, st.fox, st.foxw, st.scale, st.pre = (lambda pi, kb: v(kb)), outf, list(w), fox, list(foxw), scale, pre
            st.sm = small[:, 8 * (i % 8):8 * (i % 8) + 8]
            return st

        def turn_heads(z, nb, dst, w, last):
            tks = []
            for b0 in range(0, nb, 2):
                b = next_t()
                n = min(2, nb - b0)
                for i in range(n):
                    for t in range(2):
                        tk = tr(ps[b][:, i * 256 + t * P:i * 256 + (t + 1) * P], z(b0 + i, t), w + bfree[b],
                                inc=(i == n - 1 and t == 1))
                r = act(dst[:, b0:b0 + n, :].rearrange("p k s -> p (k s)"), ps[b][:, 0:n * 256], ACT.Copy, [tk])
                bfree[b] = [r]
                tks.append(r)
            return tks, tk

        rt_free = [None]

        def rotate(z, cos, sin, n, half, w):
            c = cos.unsqueeze(2).broadcast_to([P, 2, n, half])
            s = sin.unsqueeze(2).broadcast_to([P, 2, n, half])
            x1, x2 = z[:, :, :, 0:half], z[:, :, :, half:2 * half]
            r = [q[:, :, 0:n * half].rearrange("p t (n f) -> p t n f", f=half) for q in rt]
            w = w + [rt_free[0]]
            a = tt(r[0], x1, c, ALU.mult, w)
            b = tt(r[1], x2, s, ALU.mult, w)
            d = tt(r[2], x2, c, ALU.mult, w)
            e = tt(r[3], x1, s, ALU.mult, w)
            f = tt(x1, r[0], r[1], ALU.subtract, [a, b, e])
            g = tt(x2, r[2], r[3], ALU.add, [d, e])
            rt_free[0] = g
            return [f, g]

        zt_free = [[], []]

        ring4 = [0]

        def banks4():
            b = (ring4[0] % 4, (ring4[0] + 1) % 4)
            ring4[0] += 2
            return b

        def load_chunk(label, w):
            b = banks4()
            tk = gemm(label, b, XH, XL, 8, XW)
            last_pe[0] = tk
            return b, tk

        def mix1(l, gcol, gw):
            norm_x(gcol, None, gw)
            b, tk = load_chunk("c", 512)
            tz_ = DV.put(lambda e: e.memset(upad[:, :, 0:32], 0.0), [tk])
            for t in range(2):
                sgm = zt[0][:, t, 0:256]
                ta = act(sgm, ps[b[t]][:, 256:512], ACT.Sigmoid, [tk] + zt_free[0])
                tu = tt(zt[1][:, t, 0:256], ps[b[t]][:, 0:256], sgm, ALU.mult, [ta] + zt_free[1])
                bfree[b[t]] = [tu]
            zt_free[0] = [tu]
            bq, tkq = load_chunk("mq", 384)
            bt_ = next_t()
            for c in range(2):
                for t in range(2):
                    tk = tr(ps[bt_][:, c * 256 + t * P:c * 256 + (t + 1) * P], zt[1][:, t, c * P:(c + 1) * P],
                            [tu] + bfree[bt_], inc=(c == 1 and t == 1))
            zt_free[1] = [tk]
            tp = act(upad[:, :, 30:286], ps[bt_].rearrange("p (c s) -> p c s", c=2), ACT.Copy, [tk, tz_])
            bfree[bt_] = [tp]
            conv_tok = [[tp], [tp]]

            def conv_taps(k0, k1):
                for k in range(k0, k1):
                    for c in range(2):
                        wc = cols2[:, (2 * l + c) * 31 + k:(2 * l + c) * 31 + k + 1]
                        src = upad[:, c, k:k + 256]
                        if k == 0:
                            tk = ts(cacc[:, c, :], src, wc, cols2[:, 124 + 2 * l + c:125 + 2 * l + c], ALU.mult, ALU.add,
                                    w=conv_tok[c] + [COLS])
                        else:
                            tk = stt(cacc[:, c, :], src, wc, cacc[:, c, :], ALU.mult, ALU.add, conv_tok[c])
                        conv_tok[c] = [tk]

            def heads_in(n, b, tk, half, cos, sin, zi):
                z = zt[zi]
                r = []
                for t in range(2):
                    r.append(act(z[:, t, 0:384], ps[b[t]][:, 0:384], ACT.Copy, [tk] + zt_free[zi]))
                    bfree[b[t]] = [r[-1]]
                ro = rotate(z[:, :, 0:384].rearrange("p t (n f) -> p t n f", f=64), cos, sin, 6, half, r + [TRIG])
                return lambda: heads_out(n, zi, ro)

            def heads_out(n, zi, ro):
                z = zt[zi]
                d, tk = turn_heads(lambda i, t: z[:, t, i * P:(i + 1) * P], 3, qk1[n], ro, None)
                zt_free[zi] = [tk]
                return d

            cr, sr = cos1[:, :, 0:32], sin1[:, :, 0:32]
            cm, sm_ = cos1[:, :, 32:40], sin1[:, :, 32:40]
            fin = heads_in("mq", bq, tkq, 8, cm, sm_, 0)
            b, tk = load_chunk("mk", 384)
            rdy = {}
            rdy["mq"] = fin()
            fin = heads_in("mk", b, tk, 8, cm, sm_, 1)
            conv_taps(0, 8)
            b, tk = load_chunk("mv", 384)
            rdy["mk"] = fin()
            rdy["mv"] = [act(v1[1][:, t, :], ps[b[t]][:, 0:384], ACT.Copy, [tk]) for t in range(2)]
            for t in range(2):
                bfree[b[t]] = [rdy["mv"][t]]
            conv_taps(8, 16)
            b, tk = load_chunk("rq", 384)
            fin = heads_in("rq", b, tk, 32, cr, sr, 0)
            b, tk = load_chunk("rk", 384)
            rdy["rq"] = fin()
            fin = heads_in("rk", b, tk, 32, cr, sr, 1)
            conv_taps(16, 24)

            jobs = []
            for n in ("rv", "rg"):
                bb = banks4()
                state = dict(k=0, n=n, b=bb)
                jobs.append(state)

            def fill():
                while jobs:
                    j = jobs[0]
                    n, tk = gemm_sub(j["n"], j["b"], XH, XL, j["k"], 8, XW)
                    j["k"] += n
                    if j["k"] == 8:
                        jobs.pop(0)
                        last_pe[0] = tk
                        dst = v1[0] if j["n"] == "rv" else rg
                        rdy[j["n"]] = []
                        for t in range(2):
                            r = act(dst[:, t, :], ps[j["b"][t]][:, 0:384], ACT.Copy, [tk])
                            bfree[j["b"][t]] = [r]
                            rdy[j["n"]].append(r)
                    return

            fill()
            rdy["rk"] = fin()
            steps = []
            for h in range(6):
                lo_ = 64 * (h % 2)
                qT = qk1["mq"][lo_:lo_ + 64, h // 2, :]
                kT = qk1["mk"][lo_:lo_ + 64, h // 2, :]

                def outf(t, o, r, w, h=h):
                    return ts(ym[:, t, 384 + 64 * h:448 + 64 * h], o, r, None, ALU.mult, w=w)
                steps.append(pair_step(h, qT, kT, lambda kb, h=h: v1[1][:, kb, 64 * h:64 * h + 64], causal, outf,
                                       rdy["mq"] + rdy["mk"] + rdy["mv"]))
            attention(steps, fill)
            while jobs:
                fill()
            conv_taps(24, 31)
            srg = zt[0][:, :, 0:384]
            tsg = act(srg, rg[:, :, :], ACT.Silu, rdy["rg"] + zt_free[0])
            tks = {}
            yr = zt[1][:, :, 0:384]
            rdo = []
            for h in range(7):
                if h < 6:
                    n = nstep[0]
                    nstep[0] += 1
                    b, si_ = 4 + n % 2, n % 2
                    lo_ = 64 * (h % 2)
                    qT = qk1["rq"][lo_:lo_ + 64, h // 2, :]
                    kT = qk1["rk"][lo_:lo_ + 64, h // 2, :]
                    mm(ps[b][:, 0:256], kT[:, 0:P], qT[:, 0:256], True, True, bfree[b] + rdy["rq"] + rdy["rk"])
                    tk = mm(ps[b][:, 256:384], kT[:, P:S], qT[:, P:S], True, True, inc=True)
                    d = pt_[si_]
                    tt(d[:, 0:256], ps[b][:, 0:256], decay[:, h, :], ALU.mult, [tk, sbuf_free[si_], CST])
                    t2 = tt(d[:, 256:384], ps[b][:, 256:384], decay[:, h, 0:P], ALU.mult, [tk])
                    bfree[b] = [t2]
                    tks[h] = (si_, t2)
                if h > 0:
                    hh = h - 1
                    si_, t2 = tks[hh]
                    d = pt_[si_]
                    v = lambda kb: v1[0][:, kb, 64 * hh:64 * hh + 64]
                    o = 128 * (hh % 2)
                    mm(ps[7][:, o:o + 64], d[:, 0:P], v(0), True, True, [t2] + bfree[7] + rdy["rv"])
                    mm(ps[7][:, o + 64:o + 128], d[:, P:S], v(0), True, False)
                    tk = mm(ps[7][:, o + 64:o + 128], d[:, S:S + P], v(1), False, True, inc=True)
                    sbuf_free[si_] = tk
                    r = act(yr[:, :, 64 * hh:64 * hh + 64], ps[7][:, o:o + 128].rearrange("p (t e) -> p t e", t=2),
                            ACT.Copy, [tk] + zt_free[1])
                    bfree[7] = [r]
                    rdo.append(r)
            sqv = ym[:, :, 0:384]
            a = tt(sqv, yr, yr, ALU.mult, rdo)
            sm0 = small[:, 64:76]
            a = red(sm0, sqv.rearrange("p t (h e) -> p t h e", e=64), ALU.add, [a])
            sm1 = small[:, 76:88]
            a = ts(sm1, sm0, 1.0 / 64, EPS, ALU.mult, ALU.add, w=[a])
            sm2 = small[:, 88:100]
            a = tt(sm2, sm1, phalf[:, 0:1].broadcast_to([P, 12]), ALU.pow, [a, CST], L=PO)
            bz = tt(srg, srg, yr, ALU.mult, [tsg] + rdo)
            rb = sm2.rearrange("p (t h) -> p t h", t=2).unsqueeze(3).broadcast_to([P, 2, 6, 64])
            yret = tt(ym[:, :, 0:384].rearrange("p t (h e) -> p t h e", e=64),
                      srg.rearrange("p t (h e) -> p t h e", e=64), rb, ALU.mult, [a, bz])
            zt_free[0] = [yret]
            zt_free[1] = [bz]
            bt_ = next_t()
            for c in range(2):
                for t in range(2):
                    tk = tr(ps[bt_][:, c * 256 + t * P:c * 256 + (t + 1) * P], cacc[:, c, t * P:(t + 1) * P],
                            conv_tok[0] + conv_tok[1] + bfree[bt_], inc=(c == 1 and t == 1))
            pv = ps[bt_].rearrange("p (c t s) -> p t c s", c=2, t=2)
            r = act(yc[:, :, :].rearrange("p t (c s) -> p t c s", c=2), pv, ACT.Copy, [tk])
            bfree[bt_] = [r]
            y4 = yc[:, :, :].rearrange("p t (g e) -> p t g e", e=64)
            z4 = yc2[:, :, :].rearrange("p t (g e) -> p t g e", e=64)
            s0, s1 = small[:, 104:112], small[:, 112:120]
            bc = lambda s: s.rearrange("p (t g) -> p t g", t=2).unsqueeze(3).broadcast_to([P, 2, 4, 64])
            a = red(s0, y4, ALU.add, [r])
            a = ts(s0, s0, 1.0 / 64, None, ALU.mult, w=[a])
            a = tt(y4, y4, bc(s0), ALU.subtract, [a])
            q = tt(z4, y4, y4, ALU.mult, [a])
            q = red(s1, z4, ALU.add, [q])
            q = ts(s1, s1, 1.0 / 64, EPS, ALU.mult, ALU.add, w=[q])
            s2 = small[:, 120:128]
            q = tt(s2, s1, phalf[:, 0:1].broadcast_to([P, 8]), ALU.pow, [q], L=PO)
            a = tt(y4, y4, bc(s2), ALU.mult, [a, q])
            a = tt(yc[:, :, :], yc[:, :, :], lngb[:, l, 0, :].unsqueeze(1).broadcast_to([P, 2, 256]), ALU.mult, [a, MISC])
            a = tt(yc[:, :, :], yc[:, :, :], lngb[:, l, 1, :].unsqueeze(1).broadcast_to([P, 2, 256]), ALU.add, [a])
            yconv = act(ym[:, :, 768:1024], yc[:, :, :], ACT.Silu, [a])
            ymoba = [r for st in steps for r in st.done]
            out_x("wo", [yret, yconv] + ymoba, 1)

        def out_x(label, w, ga):
            done = turn_x(lambda k, t: ym[:, t, k * P:(k + 1) * P], w)
            for b, k, tk in done:
                split_x(b, k, tk, [last_pe[0]])
            for h in range(2):
                bb = banks4()
                tk = gemm(label, bb, XH, XL, 8, XW)
                last_pe[0] = tk
                for t in range(2):
                    add_x(t, h, bb[t], tk, ga)

        def mix2(l, s_):
            gcol = lambda k: Gc[s_ % 2][:, k:k + 1]
            scol = lambda k: shc[s_ % 2][:, k:k + 1]
            tv = norm_x(gcol, scol, ada_tok[s_])
            col_free[s_ % 2] = [tv]
            rdy = {}
            b0, tk0 = load_chunk("n0", 512)
            z = zt[0]
            r = []
            for t in range(2):
                r.append(act(z[:, t, :], ps[b0[t]], ACT.Copy, [tk0] + zt_free[0]))
                bfree[b0[t]] = [r[-1]]
            zq = z[:, :, 0:256].rearrange("p t (n f) -> p t n f", f=64)
            zk = z[:, :, 256:512].rearrange("p t (n f) -> p t n f", f=128)
            ro = rotate(zq, cos2, sin2, 4, 8, r + [CST]) + rotate(zk, cos2, sin2, 2, 8, r)
            b1, tk1 = load_chunk("n1", 140)
            z1 = zt[1]
            r1 = []
            for t in range(2):
                r1.append(act(z1[:, t, 0:140], ps[b1[t]][:, 0:140], ACT.Copy, [tk1] + zt_free[1]))
                bfree[b1[t]] = [r1[-1]]
            ro1 = rotate(z1[:, :, 0:64].rearrange("p t (n f) -> p t n f", f=64), cos2, sin2, 1, 8, r1)
            tks, tkq = turn_heads(lambda i, t: z[:, t, i * P:(i + 1) * P], 2, qn, ro, None)
            rdy["qn"] = tks

            def twice(j, src):
                return cp(dup[:, :, j, :].rearrange("p t (a f) -> p t a f", a=2),
                          src.unsqueeze(2).broadcast_to([P, 2, 2, 64]), ro + ro1)
            td = [twice(0, z[:, :, 256:320]), twice(1, z[:, :, 320:384]), twice(2, z[:, :, 384:448]),
                  twice(3, z1[:, :, 0:64])]
            rv_ = [cp(vn[:, :, 0, :], z[:, :, 448:512], r), cp(vn[:, :, 1, :], z1[:, :, 64:128], r1)]
            rdy["vn"] = rv_
            tg = cp(ng[:, :, :], z1[:, :, 128:140], r1)
            zt_free[0] = td + rv_ + [tkq]
            zt_free[1] = td + rv_ + [tg]
            kdr = []
            for j in range(4):
                b = next_t()
                for t in range(2):
                    tk = tr(ps[b][:, t * P:(t + 1) * P], dup[:, t, j, :], td + bfree[b], inc=(t == 1))
                if j < 2:
                    a1 = act(kd[0:64, j, :], ps[b][0:64, 0:256], ACT.Copy, [tk])
                    a2 = act(kd[64:128, j, 0:255], ps[b][64:128, 1:256], ACT.Copy, [tk])
                    kdr.append([a1, a2])
                else:
                    a1 = act(kd[:, j, :], ps[b][:, 0:256], ACT.Copy, [tk])
                    kdr.append([a1])
                bfree[b] = [a1] if j >= 2 else [a1, a2]
            sbuf_free[0] = sbuf_free[1] = tk

            def heads_in(b, tk, rope, zi):
                zz = zt[zi]
                r = []
                for t in range(2):
                    r.append(act(zz[:, t, 0:384], ps[b[t]][:, 0:384], ACT.Copy, [tk] + zt_free[zi]))
                    bfree[b[t]] = [r[-1]]
                if rope:
                    r = rotate(zz[:, :, 0:384].rearrange("p t (n f) -> p t n f", f=64), cos2, sin2, 6, 8, r)
                return r

            def heads_out(n, zi, r):
                zz = zt[zi]
                d, tk = turn_heads(lambda i, t: zz[:, t, i * P:(i + 1) * P], 3, qk2[n], r, None)
                zt_free[zi] = [tk]
                rdy[n] = d

            pend = None
            for i, n in enumerate(("dq", "dk", "dv", "fq", "fk", "fv")):
                b, tk = load_chunk(n, 384)
                flush()
                if pend is not None:
                    heads_out(*pend)
                    pend = None
                if n in ("dv", "fv"):
                    dst = vd if n == "dv" else vf
                    rdy[n] = []
                    for t in range(2):
                        r = act(dst[:, t, :], ps[b[t]][:, 0:384], ACT.Copy, [tk])
                        rdy[n].append(r)
                        if n == "fv":
                            r2 = act(logf[:, t, :], ps[b[t]][:, 384:390], ACT.Copy, [tk])
                            r = r2
                            rdy[n].append(r2)
                        bfree[b[t]] = [r]
                else:
                    r = heads_in(b, tk, n[0] == "d", i % 2)
                    pend = (n, i % 2, r)

            ahead_ok = [True]
            hid = small[:, 128:192].rearrange("p (v n) -> p v n", v=2)
            blk = ptT[0][:, 0:240].rearrange("p (j n) -> p j n", j=16)
            blv = ptT[1][:, 0:240].rearrange("p (j n) -> p j n", j=16)
            hs_tok = []
            tz_ = DV.put(lambda e: e.memset(small[:, 128:192], 0.0), [])
            for kv, bk in ((0, blk), (1, blv)):
                base = kd[:, kv, 0:256]
                c3_ = cols3[:, (2 * l + kv) * 16:(2 * l + kv) * 16 + 16].unsqueeze(2)
                ap = base.rearrange("p (n j b) -> p j n b", b=2, j=8)[:, :, :, 0]
                ta = tt(bk[:, 0:8, :], ap[:, :, 0:15], c3_[:, 0:8, :].broadcast_to([P, 8, 15]), ALU.add,
                        kdr[kv] + [ptT_free[kv]])
                tb2 = tt(bk[:, 8:16, :], ap[:, :, 1:16], c3_[:, 8:16, :].broadcast_to([P, 8, 15]), ALU.add, [])
                j, u, nk, un, tok = take("w1")
                wv = raw[u % NR][:, :].rearrange("p (j n) -> p j n", n=128)
                b = next_t()
                for jj in range(16):
                    tk = mm(ps[b][:, 0:15], wv[:, jj, :], bk[:, jj, :], jj == 0, jj == 15, [tok, ta, tb2] + bfree[b],
                            inc=(jj == 15))
                free_raw(u, tk)
                ptT_free[kv] = tk
                r = act(hid[:, kv, 0:15], ps[b][:, 0:15], ACT.Silu, [tk, tz_])
                bfree[b] = [r]
                hs_tok.append(r)
            ahead()
            b = next_t()
            kcT = small[:, 192:208]
            tk = mm(ps[b][:, 0:15], w2d[:, l, 0:2, :].rearrange("p a f -> p (a f)"), hid[:, 0, 0:15], True, True,
                    [hs_tok[0], MISC] + bfree[b], inc=True)
            r = cp(kcT[:, 0:15], ps[b][:, 0:15], [tk])
            hrep = ptT[0][:, 256:384].rearrange("p (h n) -> p h n", h=4)
            rr_ = cp(hrep, hid[:, 1, :].unsqueeze(1).broadcast_to([P, 4, 32]), [hs_tok[1]])
            tk = mm(ps[b][:, 64:128], ptT[0][:, 256:384], w2d[:, l, 2, :], True, True, [rr_, r], inc=True)
            vbd = ptT[1][:, 256:512]
            tzz = DV.put(lambda e: e.memset(vbd, 0.0), [ptT_free[1]])
            vb = []
            for h in range(4):
                vb.append(cp(vbd[32 * h:32 * h + 32, 64 * h:64 * h + 64], ps[b][32 * h:32 * h + 32, 64:128], [tk, tzz]))
            bfree[b] = [r] + vb
            KC = [r]

            sgn = act(ng[:, :, :], ng[:, :, :], ACT.Sigmoid, [tg])
            fb = small[:, 208:214]
            dma(SP, fb, A["fox_f_bias_2"][l].partition_broadcast(P), s_fin[0], mix_prev[0])
            n_fin[0] += 16
            lf = logf[:, :, :]
            a = tt(lf, lf, fb.unsqueeze(1).broadcast_to([P, 2, 6]), ALU.add, rdy["fv"] + [(s_fin[0], n_fin[0])])
            ab = small[:, 216:228].rearrange("p (t h) -> p t h", t=2)
            a1 = stt(ab, lf, -1.0, lf, ALU.mult, ALU.max, [a])
            a1 = act(ab, ab, ACT.Exp, [a1], scale=-1.0)
            a1 = act(ab, ab, ACT.Ln, [a1], bias=1.0)
            a2 = ts(lf, lf, 0.0, None, ALU.min, w=[a, a1])
            LF = tt(lf, lf, ab, ALU.subtract, [a2, a1])
            b = next_t()
            mm(ps[b][:, 0:6], tri[:, 0:P], logf[:, 0, :], True, True, [LF] + bfree[b])
            mm(ps[b][:, 8:14], tri[:, P:S], logf[:, 0, :], True, False)
            tk = mm(ps[b][:, 8:14], tri[:, 0:P], logf[:, 1, :], False, True, inc=True)
            cqt = cp(cq[:, :, :], ps[b][:, 0:16].rearrange("p (t n) -> p t n", t=2)[:, :, 0:6], [tk])
            bfree[b] = [cqt]

            for h in (0, 2, 1, 3):
                lo_, b = 64 * (h % 2), 4 + h % 2
                for t in range(2):
                    o = 32 * t + 16 * (h // 2)
                    tk = mm(ps[b][:, o:o + 15], qn[lo_:lo_ + 64, h // 2, t * P:(t + 1) * P],
                            kcT[lo_:lo_ + 64, 0:15], True, True, KC + rdy["qn"] + bfree[b], inc=True)
            pc = pt_[0][:, 0:256].rearrange("p (t h n) -> p t h n", t=2, h=4)
            p15 = pc[:, :, :, 0:15]
            tzz = DV.put(lambda e: e.memset(pt_[0][:, 0:256], 0.0), [sbuf_free[0]])
            cm_ = C("cmpm").rearrange("p (t n) -> p t n", t=2)
            c01 = C("cmp01").rearrange("p (t n) -> p t n", t=2)
            a = []
            for par in range(2):
                sv = ps[4 + par][:, 0:64].rearrange("p (t h n) -> p t h n", t=2, h=2)[:, :, :, 0:15]
                for t in range(2):
                    a.append(tt(p15[:, t, par::2], sv[:, t], cm_[:, t].unsqueeze(1).broadcast_to([P, 2, 15]), ALU.add,
                                [tk, tzz]))
                bfree[4 + par] = [a[-1]]
            mx8 = small[:, 64:72]
            m = red(mx8, p15, ALU.max, a)
            mb = mx8.rearrange("p (t h) -> p t h", t=2)
            a = []
            for t in range(2):
                a.append(tt(p15[:, t], p15[:, t], mb[:, t].unsqueeze(2).broadcast_to([P, 4, 15]), ALU.subtract, [m]))
            e_ = act(p15, p15, ACT.Exp, a, scale=0.125)
            a = []
            for t in range(2):
                a.append(tt(p15[:, t], p15[:, t], c01[:, t].unsqueeze(1).broadcast_to([P, 4, 15]), ALU.mult, [e_]))
            dn = small[:, 72:80]
            m = red(dn, p15, ALU.add, a)
            m = ts(dn, dn, 1e-30, None, ALU.max, w=[m])
            m = rec(dn, dn, [m])
            db = dn.rearrange("p (t h) -> p t h", t=2)
            a = []
            for t in range(2):
                a.append(tt(p15[:, t], p15[:, t], db[:, t].unsqueeze(2).broadcast_to([P, 4, 15]), ALU.mult, [m]))
            for t in range(2):
                tk = tr(ps[6][:, t * P:(t + 1) * P], pt_[0][:, t * P:(t + 1) * P], a + bfree[6], inc=(t == 1))
            sbuf_free[0] = tk
            pT = ptT[0][:, 384:640]
            r = act(pT, ps[6][:, 0:256], ACT.Copy, [tk])
            bfree[6] = [r]
            for t in range(2):
                tk = mm(ps[7][:, t * 256:(t + 1) * 256], pT[:, t * P:(t + 1) * P], vbd, True, True, [r] + vb + bfree[7], inc=(t == 1))
            ptT_free[0] = ptT_free[1] = tk
            gv = ng[:, :, :].rearrange("p t (h c) -> p t h c", c=3)
            cm1 = []
            for t in range(2):
                cm1.append(tt(ym[:, t, 0:256].rearrange("p (h e) -> p h e", e=64),
                              ps[7][:, t * 256:(t + 1) * 256].rearrange("p (h e) -> p h e", e=64),
                              gv[:, t, :, 0:1].broadcast_to([P, 4, 64]), ALU.mult, [tk, sgn]))
            bfree[7] = list(cm1)
            ycur = {(t, h): cm1 for t in range(2) for h in range(4)}

            jobs = [dict(k=0, i=i, b=None) for i in range(6)]
            gtok = []

            def fill():
                for _ in range(1):
                    if not jobs:
                        return
                    j = jobs[0]
                    if j["b"] is None:
                        j["b"] = banks4()
                    n, tk = gemm_sub("mg", j["b"], XH, XL, j["k"], 8, XW)
                    j["k"] += n
                    if j["k"] == 8:
                        jobs.pop(0)
                        last_pe[0] = tk
                        br, hf = divmod(j["i"], 2)
                        for t in range(2):
                            r = act(gts[:, t, br, 512 * hf:512 * hf + 512], ps[j["b"][t]], ACT.Copy, [tk])
                            bfree[j["b"][t]] = [r]
                            gtok.append(r)

            steps = []
            for which in range(2):
                for h in range(4):
                    lo_ = 64 * (h % 2)

                    def outf(t, o, r, w, h=h, which=which):
                        f = small[:, 80 + t:81 + t]
                        a = tt(f, r, ng[:, t, 3 * h + 1 + which:3 * h + 2 + which], ALU.mult, w + [sgn])
                        yy = ym[:, t, 64 * h:64 * h + 64]
                        q = stt(yy, o, f, yy, ALU.mult, ALU.add, [a] + ycur[t, h])
                        ycur[t, h] = [q]
                        return q
                    steps.append(pair_step(len(steps), qn[lo_:lo_ + 64, h // 2, :], kd[lo_:lo_ + 64, 2 + which, :],
                                           lambda kb, which=which: vn[:, kb, which, :], causal, outf,
                                           rdy["qn"] + kdr[2 + which] + rdy["vn"]))
            for h in range(2):
                for t in range(2):
                    st = Step()
                    st.wide = t == 1
                    w = P * (t + 1)
                    parts = []
                    for g in range(3):
                        hh = 2 * g + h
                        lo_ = 64 * (hh % 2)
                        parts.append((qk2["dq"][lo_:lo_ + 64, hh // 2, t * P:(t + 1) * P],
                                      qk2["dk"][lo_:lo_ + 64, hh // 2, 0:w], w, None))
                    mk = masks.rearrange("p g b k -> p g (b k)")
                    st.segs = [dict(t=t, o=0, parts=parts, mask=mk[:, :, P:2 * P] if t == 0 else mk)]
                    st.v = lambda pi, kb, h=h: vd[:, kb, 64 * (2 * pi + h):64 * (2 * pi + h) + 64]
                    st.out = lambda t, o, r, w, h=h: ts(ym[:, t, 256 + 64 * h:320 + 64 * h], o, r, None, ALU.mult, w=w)
                    st.w, st.fox, st.foxw, st.scale, st.pre = rdy["dq"] + rdy["dk"] + rdy["dv"], None, [], 0.125, None
                    st.sm = small[:, 8 * (len(steps) % 8):8 * (len(steps) % 8) + 8]
                    steps.append(st)
            fbuf = [zt[i][:, :, :].rearrange("p t n -> p (t n)") for i in range(2)]
            ffree = [zt_free[0], zt_free[1]]

            for h in range(6):
                lo_ = 64 * (h % 2)
                fz_ = fbuf[h % 2]
                lb = fz_[:, 0:256].rearrange("p (t q) -> p t q", t=2)
                fm = fz_[:, 256:640]
                stp = pair_step(len(steps), qk2["fq"][lo_:lo_ + 64, h // 2, :], qk2["fk"][lo_:lo_ + 64, h // 2, :],
                                lambda kb, h=h: vf[:, kb, 64 * h:64 * h + 64], None,
                                lambda t, o, r, w, h=h: ts(ym[:, t, 384 + 64 * h:448 + 64 * h], o, r, None, ALU.mult, w=w),
                                rdy["fq"] + rdy["fk"] + rdy["fv"], scale=1.0)

                def pre(st, h=h, lb=lb, fm=fm):
                    a = []
                    for t in range(2):
                        a.append(ts(lb[:, t, :], ones, logf[:, t, h:h + 1], None, ALU.mult, w=[LF] + ffree[h % 2]))
                    mm(ps[6][:, 0:256], lb[:, 0, :], tri[:, 0:256], True, False, a + bfree[6])
                    tk = mm(ps[6][:, 128:256], lb[:, 1, :], tri[:, 0:P], False, True, inc=True)
                    b1 = stt(fm[:, 0:P], ps[6][:, 0:P], cq[:, 0, h:h + 1], causal[:, P:2 * P], ALU.subtract, ALU.subtract, [tk, cqt])
                    b2 = stt(fm[:, P:3 * P], ps[6][:, 0:256], cq[:, 1, h:h + 1], causal, ALU.subtract, ALU.subtract, [tk])
                    bfree[6] = [b2]
                    st.foxw = [b1, b2]
                    ffree[h % 2] = [b2]
                stp.pre = pre
                stp.fox = lambda t, fm=fm: fm[:, 0:P] if t == 0 else fm[:, P:3 * P]
                steps.append(stp)
            attention(steps, fill)
            while jobs:
                fill()
            yall = [r for st in steps for r in st.done]
            zt_free[0] = list(yall)
            zt_free[1] = list(yall)
            tsg = act(gts[:, :, :, :].rearrange("p t b n -> p (t b n)"), gts[:, :, :, :].rearrange("p t b n -> p (t b n)"),
                      ACT.Sigmoid, gtok)
            done = turn_x(lambda k, t: ym[:, t, k * P:(k + 1) * P], yall, nk=6)
            for b, k, tk in done:
                split_x(b, k, tk, [last_pe[0]])
            mrg = []
            for hf in range(2):
                banks = [(0, 1), (2, 3), (4, 5)]
                kpos = 0
                tks = [None] * 3
                br = [(0, 0, 2), (0, 1, 2), (1, 0, 1), (2, 0, 3), (2, 1, 3), (2, 2, 3)]
                while kpos < 6:
                    j, hs, nk, un, tok = take("br")
                    for k in range(nk):
                        kk = kpos + k
                        bi, ki, kn = br[kk]
                        hi, lo = wh[hs][:, k * 512:(k + 1) * 512], wl[hs][:, k * 512:(k + 1) * 512]
                        for t in range(2):
                            bb = banks[bi][t]
                            ww = [tok] + XW(kk) + (bfree[bb] if ki == 0 else [])
                            mm(ps[bb], XH(kk, t), hi, ki == 0, False, ww)
                            mm(ps[bb], XH(kk, t), lo, False, False)
                            tk = mm(ps[bb], XL(kk, t), hi, False, ki == kn - 1, inc=(t == 1))
                        tks[bi] = tk
                    hfree[j] = tk
                    kpos += nk
                    ahead()
                last_pe[0] = tk
                for t in range(2):
                    g = lambda bi: gts[:, t, bi, 512 * hf:512 * hf + 512]
                    a = []
                    for bi in range(3):
                        a.append(tt(g(bi), ps[banks[bi][t]], g(bi), ALU.mult, [tks[bi], tsg]))
                        bfree[banks[bi][t]] = [a[-1]]
                    c_ = tt(g(0), g(0), g(1), ALU.add, [a[0], a[1]])
                    mrg.append(tt(ym[:, t, 512 * hf:512 * hf + 512], g(0), g(2), ALU.add, [c_, a[2], done[-1][2]]))
            mix_prev[0] = [mrg[-1]]
            out_x("wo2", mrg, (s_,))

        mix_prev = [[]]
        n_fin = [0, 0]
        fn_tok = [None]

        def final(gb, w, dst):
            r, sq = row_scale()
            for t in range(2):
                rd = stt(dst[:, t, :], x[:, t, :], rr[:, t:t + 1], gb, ALU.mult, ALU.mult, [r, sq] + w)
                for h in range(2):
                    xr[t, h] = [rd]
            return rd

        for si, kind in enumerate(SUBS[:stop] if stop < 99 else SUBS):
            l = (si // 3) % 2
            if kind in ("f1", "f2"):
                o = (0 if kind == "f1" else 32) + 8 * l
                if si == 5:
                    dma(SP, gaB[1][:, :], A["final_norm"].partition_broadcast(P), s_fin[1])
                    n_fin[1] += 16
                ffn(kind, lambda k: cols1[:, o + k:o + k + 1], None, [g1], None)
                if si == 5:
                    rd = final(gaB[1][:, :], [(s_fin[1], n_fin[1])], x)
                    gab_free[1] = [rd]
            elif kind == "m":
                mix1(l, lambda k: cols1[:, 16 + 8 * l + k:17 + 8 * l + k], [g1])
            else:
                s_ = si - 6
                flush()
                if kind == "M":
                    mix2(l, s_)
                else:
                    if s_ == 5:
                        dma(SP, gaB[0][:, :], A["final_norm_g_2"].partition_broadcast(P), s_fin[1], gab_free[0])
                        n_fin[1] += 16
                    ffn(kind, lambda k: Gc[s_ % 2][:, k:k + 1], lambda k: shc[s_ % 2][:, k:k + 1], ada_tok[s_], (s_,))
        if stop >= 12:
            rd = final(gaB[0][:, :], [(s_fin[1], n_fin[1])], x)
        w = [tk for v_ in xr.values() for tk in v_]
        for t in range(2):
            dma(SP, out[0, t * P:(t + 1) * P, :], x[:, t, :], s_out, w)
        SP.put(None, [(s_out, 32), MISC] + bt_all, False)

        block = ctx.enter_context(nc.Block())

        @block.sync
        def _(e):
            SP.play(e)

        @block.scalar
        def _(e):
            AC.play(e)

        @block.vector
        def _(e):
            DV.play(e)

        @block.gpsimd
        def _(e):
            PO.play(e)

        @block.tensor
        def _(e):
            PE.play(e)


_INS = ["x", "positions", "ffn1_norm", "ffn1_wg", "ffn1_wu", "ffn1_wd", "mix_norm", "w_in", "conv_w", "conv_b",
        "conv_ln_g", "conv_ln_b", "w_out", "ffn2_norm", "ffn2_wg", "ffn2_wu", "ffn2_wd", "final_norm", "c_2",
        "ada_w_2", "ada_b_2", "norm_g_2", "final_norm_g_2", "ffn_w_in_2", "ffn_w_out_2", "mix_w_in_2",
        "nsa_cmp_pe_2", "nsa_cmp_w1_2", "nsa_cmp_w2_2", "fox_f_bias_2", "br_w_nsa_2", "br_w_dil_2", "br_w_fox_2",
        "mix_w_out_2"]


def kernel(**inputs):
    import concourse.bacc as _bacc
    from concourse.bass_utils import run_bass_kernel_spmd as _run

    nc = _bacc.Bacc("TRN2", target_bir_lowering=False, num_devices=1)
    arrays, A = {}, {}
    given = {n: np.ascontiguousarray(inputs[n]) for n in _INS}
    given["cst"] = constants()
    for name, a in given.items():
        arrays[f"in_{name}"] = a
        A[name] = nc.dram_tensor(f"in_{name}", a.shape, mybir.dt.from_np(a.dtype), kind="ExternalInput").ap()
    out = nc.dram_tensor("out_0", (1, S, D), F32, kind="ExternalOutput").ap()
    program(nc, A, out)
    r = _run(nc, [arrays], core_ids=[0])
    return r.results[0]["out_0"]
```

```python
import concourse.bass as bass
from concourse import mybir
import numpy as np
from contextlib import ExitStack

F32 = mybir.dt.float32
F32R = mybir.dt.float32r
I32 = mybir.dt.int32
ALU = mybir.AluOpType
ACT = mybir.ActivationFunctionType
AX = mybir.AxisListType

P = 128
D = 1024
FF = 2816
S = 256
NEG = -1e30
EPS = 1e-6

CONST_PARTS = [("ident", 128), ("ones", 128), ("phalf", 2), ("masks", 3 * 256), ("causal", 256), ("decay", 6 * 256),
               ("tri", 256), ("cos2", 16), ("sin2", 16), ("inv", 40), ("cmpm", 30), ("cmp01", 30)]


def const_cols():
    at, out = 0, {}
    for name, n in CONST_PARTS:
        out[name] = (at, n)
        at += n
    return out, at


def constants():
    cols, n = const_cols()
    c = np.zeros((P, n), np.float32)

    def put(name, a):
        o, w = cols[name]
        c[:, o:o + w] = np.asarray(a, np.float32).reshape(P, w)

    i = np.arange(P)[:, None]
    j = np.arange(P)[None, :]
    put("ident", np.eye(P))
    put("ones", np.ones((P, P)))
    m = np.zeros((P, 3, 2, P))
    for g, dil in enumerate((1, 4, 16)):
        off = (j >= i) if g == 0 else ((i - j) % dil == 0)
        m[:, g, 0] = np.where(off, 0.0, NEG)
        m[:, g, 1] = np.where((j <= i) & ((i - j) % dil == 0), 0.0, NEG)
    put("masks", m)
    cm = np.zeros((P, 2, P))
    cm[:, 1] = np.where(j <= i, 0.0, NEG)
    put("causal", cm)
    f = np.float32
    lg = np.log1p(-np.exp2(f(-5.0) - np.arange(6, dtype=np.float32))).astype(np.float32)
    dec = np.zeros((P, 6, 2 * P), np.float32)
    rel = np.arange(2 * P, dtype=np.float32)[None, :] - np.arange(P, dtype=np.float32)[:, None]
    for h in range(6):
        dec[:, h] = np.where(rel >= 0, np.exp(lg[h] * np.maximum(rel, f(0))), 0.0) * f(0.125)
    put("decay", dec)
    t = np.ones((P, 2, P))
    t[:, 0] = i <= j
    put("tri", t)
    inv2 = (f(500000.0) ** (-np.arange(0, 16, 2, dtype=np.float32) / f(16))).astype(np.float32)
    pos = np.arange(2, dtype=np.float32)[None, :, None] * f(128) + np.arange(P, dtype=np.float32)[:, None, None]
    ang = (pos * inv2).astype(np.float32)
    put("cos2", np.cos(ang))
    put("sin2", np.sin(ang))
    ret = (f(10000.0) ** (-np.linspace(0.0, 1.0, 32, dtype=np.float32))).astype(np.float32)
    rope = (f(500000.0) ** (-np.arange(8, dtype=np.float32) / f(8))).astype(np.float32)
    put("inv", np.broadcast_to(np.concatenate([ret, rope]), (P, 40)))
    ends = np.arange(15) * 16 + 31
    ok = ends[None, None, :] <= (np.arange(2)[None, :, None] * 128 + np.arange(P)[:, None, None])
    put("cmpm", np.where(ok, 0.0, NEG))
    put("cmp01", ok)
    c[:, cols["phalf"][0]] = -0.5
    c[:, cols["phalf"][0] + 1] = np.pi / 2
    return c


class Line:

    def __init__(self, sem):
        self.sem, self.n, self.items = sem, 0, []

    def put(self, fn, waits, inc=True):
        self.items.append((fn, [w for w in waits if w is not None], inc))
        if inc:
            self.n += 1
            return (self.sem, self.n)
        return None

    def put_dma(self, fn, waits, sem):
        self.items.append((fn, [w for w in waits if w is not None], sem))

    def play(self, eng):
        seen = {}
        for fn, waits, inc in self.items:
            for sem, v in waits:
                if seen.get(id(sem), 0) < v:
                    eng.wait_ge(sem, v)
                    seen[id(sem)] = v
            if fn is None:
                continue
            ins = fn(eng)
            if inc is True:
                ins.then_inc(self.sem, 1)
            elif inc is not False:
                ins.then_inc(inc, 16)


NR = 4
NH = 5
LA = 3
AGE = 3
LAG = 3
ADA_BY = [20, 32, 32, 52, 68, 68, 72]


def program(nc, A, out, dbg=None, stop=99):
    ctx = ExitStack()
    with ctx:
        top = [(nc.sbuf_base + 63) // 64 * 64]

        def place(name, shape, dt, at):
            return nc.alloc_sbuf_tensor_at(name, shape, dt, offset=at)

        def size(shape):
            n = 4
            for s in shape[1:]:
                n *= s
            return (n + 31) // 32 * 32

        def sb(name, shape, dt=F32):
            t = place(name, shape, dt, top[0])
            top[0] += size(shape)
            return t

        def sem(name):
            return ctx.enter_context(nc.semaphore(name))

        cols, NC = const_cols()
        cst = sb("cst", [P, NC])

        def C(name):
            o, w = cols[name]
            return cst[:, o:o + w]

        ident = C("ident")
        ones = C("ones")
        masks = C("masks").rearrange("p (g b k) -> p g b k", g=3, b=2)
        causal = C("causal")
        decay = C("decay").rearrange("p (h c) -> p h c", h=6)
        tri = C("tri")
        phalf = C("phalf")
        cos2 = C("cos2").rearrange("p (t f) -> p t f", t=2)
        sin2 = C("sin2").rearrange("p (t f) -> p t f", t=2)

        x = sb("x", [P, 2, D])
        xh = sb("xh", [P, 8, S], F32R)
        xl = sb("xl", [P, 8, S], F32R)
        raw = [sb(f"raw{i}", [P, 2048]) for i in range(NR)]
        wh = [sb(f"wh{i}", [P, 1024], F32R) for i in range(NH)]
        wl = [sb(f"wl{i}", [P, 1024], F32R) for i in range(NH)]
        cols1 = sb("cols1", [P, 104])
        cols2 = sb("cols2", [P, 128])
        cols3 = sb("cols3", [P, 64])
        condT = sb("condT", [P, 8])
        w2d = sb("w2d", [P, 2, 3, 64])
        cos1 = sb("cos1", [P, 2, 40])
        sin1 = sb("sin1", [P, 2, 40])
        gaB = [sb(f"gaB{i}", [P, D]) for i in range(2)]
        lngb = place("lngb", [P, 2, 2, 256], F32, top[0])
        acc = [sb(f"acc{i}", [P, 512]) for i in range(2)]
        bt = [sb(f"bt{i}", [P, 512]) for i in range(2)]
        shc = [sb(f"shc{i}", [P, 8]) for i in range(2)]
        Gc = [sb(f"Gc{i}", [P, 8]) for i in range(2)]
        ssq = sb("ssq", [P, 4])
        ms = sb("ms", [P, 8])
        rr = sb("rr", [P, 2])
        U0 = top[0]
        END = [U0]

        def region(start):
            cur = [start]

            def put(name, shape, dt=F32):
                t = place(name, shape, dt, cur[0])
                cur[0] += size(shape)
                END[0] = max(END[0], cur[0])
                return t
            return put, cur

        fz, fcur = region(U0)
        hTh = fz("hTh", [P, 22, S], F32R)
        hTl = fz("hTl", [P, 22, S], F32R)
        sg = [fz(f"sg{i}", [P, 512]) for i in range(2)]
        hb = [[fz(f"hb{i}{t}", [P, 512]) for t in range(2)] for i in range(2)]
        nz, _ = region(fcur[0])
        vT = nz("vT", [P, 8, S])
        junk = nz("junk", [P, 512])
        dg = nz("dg", [P, S])
        mz, mcur = region(U0)
        zt = [mz(f"zt{i}", [P, 2, 512]) for i in range(2)]
        dup = place("dup", [P, 2, 4, 128], F32, mcur[0])
        pt_ = [mz(f"pt{i}", [P, 768]) for i in range(2)]
        ptT = [mz(f"ptT{i}", [P, 768]) for i in range(2)]
        ym = mz("ym", [P, 2, D])
        small = mz("small", [P, 256])
        m0 = mcur[0]
        yh = place("yh", [P, 8, S], F32R, U0)
        yl = place("yl", [P, 8, S], F32R, U0 + 8192)
        m1, m1cur = region(m0)
        rv = m1("rv", [P, 2, 384])
        rg = m1("rg", [P, 2, 384])
        qk1 = {n: m1("T" + n, [P, 3, S]) for n in ("rq", "rk")}
        cacc = m1("cacc", [P, 2, S])
        yc = m1("yc", [P, 2, 256])
        yc2 = m1("yc2", [P, 2, 256])
        y1h = place("y1h", [P, 8, S], F32R, m1cur[0])
        y1l = place("y1l", [P, 8, S], F32R, m1cur[0] + 8192)
        mv = m1("mv", [P, 2, 384])
        qk1.update((n, m1("T" + n, [P, 3, S])) for n in ("mq", "mk"))
        rt1 = [m1(f"rt1{i}", [P, 2, 192]) for i in range(4)]
        upad = m1("upad", [P, 2, 288])
        m2, _ = region(m0)
        w1b = [place(f"w1b{i}", [P, 2048], F32, m0 + 8192 * i) for i in range(2)]
        gts = m2("gts", [P, 2, 3, D])
        qk2 = {n: m2("T" + n, [P, 3, S]) for n in ("dq", "dk", "fq", "fk")}
        qn = m2("qn", [P, 2, S])
        kd = m2("kd", [P, 4, S])
        vn = m2("vn", [P, 2, 2, 64])
        vd = m2("vd", [P, 2, 384])
        vf = m2("vf", [P, 2, 384])
        ng = m2("ng", [P, 2, 12])
        logf = m2("logf", [P, 2, 6])
        cq = m2("cq", [P, 2, 6])
        rt2 = [m2(f"rt2{i}", [P, 2, 48]) for i in range(4)]
        assert END[0] <= nc.sbuf_usable_end, (END[0], nc.sbuf_usable_end)

        ps = [ctx.enter_context(nc.psum_tensor(f"ps{i}", [P, 512], F32)) for i in range(4)]
        s45 = ctx.enter_context(nc.psum_tensor("s45", [P, 1024], F32))
        ps += [s45[:, 0:512], s45[:, 512:1024]]
        ps += [ctx.enter_context(nc.psum_tensor(f"ps{i}", [P, 512], F32)) for i in range(6, 8)]
        ps = [p[:, :] for p in ps]

        PE, AC, DV, PO, SP = (Line(sem(n)) for n in ("s_pe", "s_act", "s_dve", "s_pool", "s_sp"))
        s_raw = [sem(f"s_raw{i}") for i in range(NR)]
        n_raw = [0] * NR
        s_bt = [sem(f"s_bt{i}") for i in range(2)]
        n_bt = [0] * 2
        s_cst = sem("s_cst")
        s_rows = sem("s_rows")
        s_x = [sem("s_x0"), sem("s_x1")]
        s_cst0 = sem("s_cst0")
        s_rows2 = sem("s_rows2")
        s_misc = sem("s_misc")
        s_w1 = [sem("s_w10"), sem("s_w11")]
        s_fin = [sem("s_fin0"), sem("s_fin1")]
        s_out = sem("s_out")

        def mm(o, l, r, start, stop, w=(), inc=False):
            return PE.put(lambda e: e.matmul(o, l, r, start=start, stop=stop), w, inc)

        def tr(o, i, w=(), inc=False):
            n = i.shape[0]
            return PE.put(lambda e: e.transpose(o, i, ident[0:n, 0:n]), w, inc)

        def act(o, i, f, w=(), **kw):
            return AC.put(lambda e: e.activation(o, i, f, **kw), w)

        def tt(o, a, b, op, w=(), L=None):
            return (L or DV).put(lambda e: e.tensor_tensor(o, a, b, op), w)

        def ts(o, a, s1, s2, op0, op1=None, w=(), L=None):
            if op1 is None:
                return (L or DV).put(lambda e: e.tensor_scalar(o, a, s1, None, op0), w)
            return (L or DV).put(lambda e: e.tensor_scalar(o, a, s1, s2, op0, op1), w)

        def stt(o, a, s, b, op0, op1, w=()):
            return DV.put(lambda e: e.scalar_tensor_tensor(out=o, in0=a, scalar=s, in1=b, op0=op0, op1=op1), w)

        def cp(o, a, w=(), L=None):
            return (L or DV).put(lambda e: e.tensor_copy(o, a), w)

        def red(o, a, op, w=()):
            return DV.put(lambda e: e.tensor_reduce(o, a, AX.X, op), w)

        def rec(o, a, w=()):
            return DV.put(lambda e: e.reciprocal(o, a), w)

        def ttr(o, a, b, red_, w=()):
            return DV.put(lambda e: e.tensor_tensor_reduce(o, a, b, 1.0, -3e38, ALU.add, ALU.max, red_), w)

        def dma(L, o, i, s, w=()):
            L.put_dma(lambda e: e.dma_start(o, i), w, s)

        units = []

        def wview(W, k0, nk, c0, w):
            return W[k0 * P:(k0 + nk) * P, c0:c0 + w].rearrange("(k p) n -> p k n", p=P)

        def add_gemm(label, W, K, c0, w):
            nk = 4 if w > 256 else 8
            for k0 in range(0, K, nk):
                n = min(nk, K - k0)
                units.append(dict(kind="w", label=label, nk=n, w=w, per=2 if w > 256 else 4,
                                  src=[(wview(W, k0, n, c0, w), 0, w)]))

        def add_ada(upto, a, b):
            n = upto - ada_at[0]
            for m in range(n):
                q, half = divmod(ada_at[0], 2)
                s_, i = divmod(q, 6)
                l, j = divmod(s_, 3)
                W = A["ada_w_2"][l]
                units.insert(a + (b - a) * (2 * m + 1) // (2 * n) + m, dict(
                    kind="a", label=None, nk=4, w=512, q=q, half=half,
                    src=[(wview(W, 4 * half, 4, (6 * j + i) * 512, 512), 0, 512)]))
                ada_at[0] += 1

        ada_at = [0]

        def plan_ffn(label, Wg, g0, Wu, f0, Wd, ada):
            u0 = len(units)
            for c in range(6):
                if c < 5:
                    add_gemm(label + "g", Wg, 8, g0 + 512 * c, 512)
                    add_gemm(label + "u", Wu, 8, f0 + 512 * c, 512)
                else:
                    for k0 in (0, 4):
                        units.append(dict(kind="w", label=label + "gu", nk=4, w=512, per=2, src=[
                            (wview(Wg, k0, 4, g0 + 2560, 256), 0, 256), (wview(Wu, k0, 4, f0 + 2560, 256), 256, 256)]))
            for h in range(2):
                add_gemm(label + "d", Wd, 22, 512 * h, 512)
            add_ada(ada, u0 + 1, len(units) - 6)

        L1CH = [("c", 2688, 512), ("mq", 1536, 384), ("mk", 1920, 384), ("mv", 2304, 384),
                ("rq", 0, 384), ("rk", 384, 384), ("rv", 768, 384), ("rg", 1152, 384)]
        L2CH = [("n0", 0, 512), ("n1", 512, 140), ("dq", 652, 384), ("dk", 1036, 384), ("dv", 1420, 384),
                ("fq", 1804, 384), ("fk", 2188, 384), ("fv", 2572, 390)]
        ADA = [0] * 5 + ADA_BY
        SUBS = ["f1", "m", "f2"] * 2 + ["F1", "M", "F2"] * 2
        for si, kind in enumerate(SUBS[:stop] if stop < 99 else SUBS):
            l = (si // 3) % 2
            if kind in ("f1", "f2"):
                n = "ffn" + kind[1]
                plan_ffn(kind, A[n + "_wg"][l], 0, A[n + "_wu"][l], 0, A[n + "_wd"][l], ADA[si])
            elif kind == "m":
                for n, c0, w in L1CH:
                    add_gemm(n, A["w_in"][l], 8, c0, w)
                W = A["w_out"][l]
                for k0, k1 in ((3, 4), (5, 6), (7, 0), (1, 2)):
                    units.append(dict(kind="w", label="wo", nk=4, w=512, per=2, src=[
                        (wview(W, k, 1, 512 * h, 512), 0, 512, 2 * h + i, 2 * h + i + 1)
                        for h in range(2) for i, k in enumerate((k0, k1))]))
            elif kind in ("F1", "F2"):
                b = int(kind[1]) - 1
                W = A["ffn_w_in_2"][l, b]
                plan_ffn(kind, W, 0, W, FF, A["ffn_w_out_2"][l, b], ADA[si])
            else:
                W = A["mix_w_in_2"][l]
                for i, (n, c0, w) in enumerate(L2CH):
                    add_gemm(n, W, 8, c0, w)
                for b in range(6):
                    add_gemm("mg", W, 8, 2962 + 512 * b, 512)
                for h in range(2):
                    units.append(dict(kind="w", label="br", nk=3, w=512, per=2, src=[
                        (wview(A["br_w_nsa_2"][l], 0, 2, 512 * h, 512), 0, 512, 0, 2),
                        (wview(A["br_w_dil_2"][l], 0, 1, 512 * h, 512), 0, 512, 2, 3)]))
                    add_gemm("br", A["br_w_fox_2"][l], 3, 512 * h, 512)
                for k0 in (0, 4):
                    for h in range(2):
                        units.append(dict(kind="w", label="wo2", nk=4, w=512, per=2,
                                          src=[(wview(A["mix_w_out_2"][l], k0, 4, 512 * h, 512), 0, 512)]))
                add_ada(ADA[si], len(units) - 20, len(units) - 8)

        subs = []
        for u, un in enumerate(units):
            if un["kind"] == "w":
                for k0 in range(0, un["nk"], un["per"]):
                    subs.append((u, k0, min(un["per"], un["nk"] - k0)))
            else:
                subs.append((u, 0, un["nk"]))

        issued = [0]
        raw_tok = {}
        raw_done = {}

        def issue(u):
            if u >= len(units):
                return
            assert u == issued[0]
            issued[0] += 1
            un, slot = units[u], u % NR
            view = raw[slot][:, 0:un["nk"] * un["w"]].rearrange("p (k n) -> p k n", n=un["w"])
            for piece in un["src"]:
                src, c0, w = piece[:3]
                k0, k1 = piece[3:] if len(piece) > 3 else (0, un["nk"])
                dma(SP, view[:, k0:k1, c0:c0 + w], src, s_raw[slot], raw_done.get(u - NR, ()))
                n_raw[slot] += 16
            raw_tok[u] = (s_raw[slot], n_raw[slot])

        bfree = [[] for _ in range(8)]
        made = [0]
        wsub = [0]
        ready = {}
        hfree = {}
        cond_tok = [None]
        bt_ready = [None] * 2
        bt_all = []
        accr = [[], []]
        reduces = []
        reduced = [-1]
        gab_free = [[], []]
        col_free = [[], []]
        ada_tok = {}
        macs = {}

        def bt_issue(q, w):
            if q >= 36:
                return
            s_, i = divmod(q, 6)
            l, j = divmod(s_, 3)
            o = (6 * j + i) * 512
            dma(SP, bt[q % 2][0:1, :], A["ada_b_2"][l:l + 1, o:o + 512], s_bt[q % 2], w)
            n_bt[q % 2] += 16
            bt_ready[q % 2] = (s_bt[q % 2], n_bt[q % 2])
            bt_all.append(bt_ready[q % 2])

        def make():
            u, k0, nk = subs[made[0]]
            un, slot = units[u], u % NR
            made[0] += 1
            last = made[0] == len(subs) or subs[made[0]][0] != u
            if un["kind"] == "w":
                j = wsub[0]
                wsub[0] += 1
                hs = j % NH
                n = nk * un["w"]
                src = raw[slot][:, k0 * un["w"]:k0 * un["w"] + n]
                hi, lo = wh[hs][:, 0:n], wl[hs][:, 0:n]
                free = hfree.get(j - NH)
                th = act(hi, src, ACT.Copy, [raw_tok[u], free])
                tl = tt(lo, src, hi.bitcast(F32), ALU.subtract, [raw_tok[u], th, free])
                ready[j] = (hs, nk, un, tl)
                if last:
                    raw_done[u] = [tl]
                    issue(u + NR)
            else:
                q = un["q"]
                a = acc[q % 2]
                for k in range(4):
                    kk = 4 * un["half"] + k
                    wl_ = [raw_tok[u], cond_tok[0]]
                    if kk == 0:
                        if reduced[0] < q - 2:
                            flush()
                        prev = bt[q % 2][:, :]
                        wl_ += [bt_ready[q % 2]] + accr[q % 2]
                    else:
                        prev = a[:, :]
                        wl_ += [macs[q]]
                    t = stt(a[:, :], raw[slot][:, k * 512:k * 512 + 512], condT[:, kk:kk + 1], prev,
                            ALU.mult, ALU.add, wl_)
                    macs[q] = t
                    if kk == 0:
                        bt_issue(q + 2, [t])
                raw_done[u] = [t]
                issue(u + NR)
                if un["half"]:
                    reduces.append((q, t, taken[0]))

        taken = [0]

        def take(label):
            j = taken[0]
            taken[0] += 1
            while wsub[0] <= j:
                make()
            hs, nk, un, tok = ready.pop(j)
            assert un["label"] == label, (un["label"], label)
            return j, hs, nk, un, tok

        def ahead():
            while wsub[0] < taken[0] + LA and made[0] < len(subs):
                make()

        def flush(age=0):
            while reduces and reduces[0][2] + age <= taken[0]:
                q, tok, _ = reduces.pop(0)
                reduce_mod(q, tok)
                reduced[0] = q

        tbank = [6]

        def next_t():
            tbank[0] = 13 - tbank[0]
            return tbank[0]

        def reduce_mod(q, tok):
            s_, i = divmod(q, 6)
            a, b = acc[q % 2], next_t()
            if i < 4:
                t = mm(ps[b], ones, a[:, :], True, True, [tok] + bfree[b], inc=True)
                v = ps[b].rearrange("p (k n) -> p k n", n=P)
                r = tt(v, v, ident.unsqueeze(1).broadcast_to([P, 4, P]), ALU.mult, [t])
                o = 4 * (i % 2)
                if i < 2:
                    r = red(shc[s_ % 2][:, o:o + 4], v, ALU.add, [r] + col_free[s_ % 2])
                    bfree[b] = [r]
                else:
                    g = cols1[:, 48 + 8 * s_ + o:48 + 8 * s_ + o + 4]
                    r = red(ms[:, 4:8], v, ALU.add, [r])
                    bfree[b] = [r]
                    r = stt(Gc[s_ % 2][:, o:o + 4], ms[:, 4:8], 1.0, g, ALU.add, ALU.mult, [r] + col_free[s_ % 2])
            else:
                t = mm(ps[b], ones, a[:, :], True, True, [tok] + bfree[b], inc=True)
                o = 512 * (i - 4)
                r = act(gaB[s_ % 2][:, o:o + 512], ps[b], ACT.Copy, [t] + gab_free[s_ % 2],
                        scale=1.0 if s_ % 3 == 1 else 0.5)
                bfree[b] = [r]
            accr[q % 2] = [t]
            ada_tok.setdefault(s_, []).append(r)

        def gemm_sub(label, banks, hiT, loT, kpos, K, xw):
            j, hs, nk, un, tok = take(label)
            w = un["w"]
            for k in range(nk):
                kk = kpos + k
                hi, lo = wh[hs][:, k * w:(k + 1) * w], wl[hs][:, k * w:(k + 1) * w]
                for t in range(2):
                    b = banks[t]
                    o = ps[b][:, 0:w]
                    a, c = hiT(kk, t), loT(kk, t)
                    ww = [tok] + xw(kk)
                    if kk == 0:
                        ww += bfree[b]
                    end = kk == K - 1
                    mm(o, a, hi, kk == 0, False, ww)
                    mm(o, a, lo, False, False)
                    t_ = mm(o, c, hi, False, end, inc=(k == nk - 1 and t == 1))
            hfree[j] = t_
            ahead()
            return nk, t_

        def gemm(label, banks, hiT, loT, K, xw):
            k = 0
            while k < K:
                n, t = gemm_sub(label, banks, hiT, loT, k, K, xw)
                k += n
            return t

        XH = lambda k, t: xh[:, k, t * P:(t + 1) * P]
        XL = lambda k, t: xl[:, k, t * P:(t + 1) * P]
        x_ready = {}

        def XW(k):
            return x_ready[k]

        rows = fcur[0] + 8192 + 2048 + 1024
        assert rows + 3600 <= nc.sbuf_usable_end
        rows1 = place("rows1", [P, 128], F32, rows)
        rows2 = place("rows2", [P, 128], F32, rows + 512)
        rows3 = place("rows3", [P, 128], F32, rows + 1024)
        posi = place("posi", [P, 128], I32, rows + 1536)
        posr = place("posr", [P, 128], F32, rows + 2048)
        posf = place("posf", [P, 2], F32, rows + 2560)
        an = [place(f"an{i}", [P, 2, 40], F32, rows + 2592 + 320 * i) for i in range(3)]

        dma(SP, x[:, 0, :], A["x"][0, 0:P, :], s_x[0])
        X0 = [(s_x[t], 16) for t in range(2)]
        dma(AC, cst[:, 0:258], A["cst"][:, 0:258], s_cst0)
        o = 0
        for n, k in (("ffn1_norm", 16), ("mix_norm", 16), ("ffn2_norm", 16)):
            dma(AC, rows1[o:o + k, :], A[n].rearrange("l (k p) -> (l k) p", p=P), s_rows)
            o += k
        dma(SP, rows1[48:96, :], A["norm_g_2"].rearrange("l s (k p) -> (l s k) p", p=P), s_rows)
        dma(AC, rows1[96:104, :], A["c_2"].rearrange("a (k p) -> (a k) p", p=P), s_rows)
        dma(SP, x[:, 1, :], A["x"][0, P:S, :], s_x[1])
        CST0, ROWS1 = (s_cst0, 16), (s_rows, 80)
        for u in range(NR):
            issue(u)
        t = tr(ps[5][:, 0:104], rows1[0:104, :], [CST0, ROWS1], inc=True)
        g1 = cp(cols1[:, :], ps[5][:, 0:104], [t])
        bfree[5] = [g1]

        dma(AC, cst[:, 258:NC], A["cst"][:, 258:NC], s_cst)
        nrow = 0
        for l in range(2):
            for c in range(2):
                o = (2 * l + c) * 31
                dma(AC, rows2[o:o + 31, :], A["conv_w"][l, :, c * P:(c + 1) * P], s_rows2)
                nrow += 1
        dma(AC, rows2[124:128, :], A["conv_b"].rearrange("l (c p) -> (l c) p", p=P), s_rows2)
        dma(AC, rows3[0:64, :], A["nsa_cmp_pe_2"].rearrange("l v (j b) d -> (l v j) (b d)", b=2), s_rows2)
        dma(AC, posi[0:2, :], A["positions"].rearrange("a (t p) -> (a t) p", p=P), s_rows2)
        nrow += 3
        n_misc = 0
        for l in range(2):
            for a, b in ((0, 0), (0, 1), (1, 2)):
                dma(AC, w2d[:, l, b, :], A["nsa_cmp_w2_2"][l, a], s_misc)
                n_misc += 16
            dma(AC, lngb[:, l, 0, :], A["conv_ln_g"][l].partition_broadcast(P), s_misc)
            dma(AC, lngb[:, l, 1, :], A["conv_ln_b"][l].partition_broadcast(P), s_misc)
            n_misc += 32
        CST, ROWS, MISC = (s_cst, 16), (s_rows2, 16 * nrow), (s_misc, n_misc)
        TRIG = [None]

        def setup_rest():
            b = next_t()
            t = tr(ps[b][:, 0:128], rows2[:, :], [ROWS] + bfree[b], inc=True)
            bfree[b] = [cp(cols2[:, :], ps[b][:, 0:128], [t])]
            b = next_t()
            t = tr(ps[b][:, 0:64], rows3[0:64, :], bfree[b], inc=True)
            bfree[b] = [cp(cols3[:, :], ps[b][:, 0:64], [t])]
            cond_tok[0] = act(condT[:, :], cols1[:, 96:104], ACT.Silu, [g1])
            inv = C("inv")
            t = cp(posr[0:2, :], posi[0:2, :], [ROWS])
            b = next_t()
            t = tr(ps[b][:, 0:2], posr[0:2, :], [t] + bfree[b], inc=True)
            t = cp(posf[:, :], ps[b][:, 0:2], [t])
            bfree[b] = [t]
            for i in range(2):
                ta = ts(an[0][:, i, :], inv, posf[:, i:i + 1], None, ALU.mult, w=[t, CST])
            magic = 12582912.0
            a0, a1, a2 = an[0][:, :, :], an[1][:, :, :], an[2][:, :, :]
            q = ts(a1, a0, float(np.float32(1 / (2 * np.pi))), magic, ALU.mult, ALU.add, w=[ta])
            q = ts(a1, a1, -magic, None, ALU.add, w=[q])
            c1 = 6.28125
            c2 = float(np.float32(round((2 * np.pi - c1) * 2 ** 21) / 2 ** 21))
            c3 = float(np.float32(2 * np.pi - c1 - c2))
            for cc in (c1, c2, c3):
                q = stt(a0, a1, -cc, a0, ALU.mult, ALU.add, [q])
            pi_ = float(np.nextafter(np.float32(np.pi), np.float32(0)))
            q = ts(a0, a0, pi_, -pi_, ALU.min, ALU.max, w=[q])
            q2 = stt(a2, a0, -1.0, a0, ALU.mult, ALU.max, [q])
            act(sin1[:, :, :], a0, ACT.Sin, [q])
            TRIG[0] = act(cos1[:, :, :], a2, ACT.Sin, [q2, CST], scale=-1.0, bias=phalf[:, 1:2])
            tz = [DV.put(lambda e, i=i: e.memset(bt[i][:, :], 0.0), []) for i in range(2)]
            bt_issue(0, [tz[0]])
            bt_issue(1, [tz[1]])

        xr = {(t, h): [X0[t]] for t in range(2) for h in range(2)}
        sq_tok = {}
        junk_free = [None]

        def square(t, h):
            sq_tok[t, h] = act(junk[:, :], x[:, t, h * 512:(h + 1) * 512], ACT.Square, xr[t, h] + [junk_free[0]],
                               accum_out=ssq[:, 2 * h + t:2 * h + t + 1])
            junk_free[0] = sq_tok[t, h]

        def row_scale():
            a = tt(ms[:, 0:2], ssq[:, 0:2], ssq[:, 2:4], ALU.add, [sq_tok[t, h] for t in range(2) for h in range(2)])
            a = ts(ms[:, 2:4], ms[:, 0:2], 1.0 / D, EPS, ALU.mult, ALU.add, w=[a])
            r_tok[0] = tt(rr[:, :], ms[:, 2:4], phalf[:, 0:1].broadcast_to([P, 2]), ALU.pow, [a, CST0], L=PO)

        r_tok = [None]

        def prep(h, nx):
            bb = (next_t(), next_t())
            tks = [None, None]
            for t in range(2):
                for n in range(2):
                    for kk in range(2):
                        k = 4 * h + 2 * n + kk
                        tks[n] = tr(ps[bb[n]][:, kk * 256 + t * P:kk * 256 + (t + 1) * P], x[:, t, k * P:(k + 1) * P],
                                    xr[t, h] + bfree[bb[n]], inc=(kk == 1 and t == 1))
            for n in range(2):
                k, b, tk = 4 * h + 2 * n, bb[n], tks[n]
                if nx[0] == "plain":
                    for kk in range(2):
                        g = nx[1](k + kk)
                        i = ps[b][:, kk * 256:(kk + 1) * 256]
                        th = act(xh[:, k + kk, :], i, ACT.Copy, [tk] + nx[2], scale=g)
                        if kk:
                            th1 = th
                    for kk in range(2):
                        g = nx[1](k + kk)
                        i = ps[b][:, kk * 256:(kk + 1) * 256]
                        tl = stt(xl[:, k + kk, :], i, g, xh[:, k + kk, :].bitcast(F32), ALU.mult, ALU.subtract, [th1])
                    bfree[b] = [tl]
                    x_ready[k] = x_ready[k + 1] = [tl]
                else:
                    s_ = nx[1]
                    assert len(ada_tok[s_]) >= 4
                    o = vT[:, k:k + 2, :]
                    i = ps[b].rearrange("p (k s) -> p k s", k=2)
                    if k % 4:
                        r = tt(o, i, Gc[s_ % 2][:, k:k + 2].unsqueeze(2).broadcast_to([P, 2, S]), ALU.mult,
                               [tk] + ada_tok[s_])
                    else:
                        for kk in range(2):
                            r = act(o[:, kk], i[:, kk], ACT.Copy, [tk] + ada_tok[s_],
                                    scale=Gc[s_ % 2][:, k + kk:k + kk + 1])
                    bfree[b] = [r]
                    v_ready[k // 2] = r

        v_ready = {}

        def finish(nx):
            s_ = nx[1]
            b = next_t()
            for t in range(2):
                a = ts(dg[:, t * P:(t + 1) * P], ident, rr[:, t:t + 1], None, ALU.mult, w=[r_tok[0]])
            tk = mm(ps[b][:, 0:S], ones, dg[:, :], True, True, [a] + bfree[b], inc=True)
            sc = lambda k: shc[s_ % 2][:, k:k + 1]
            th = {}
            for k in range(9):
                if k < 8:
                    u = tt(vT[:, k, :], vT[:, k, :], ps[b][:, 0:S], ALU.mult, [tk, v_ready[k // 2]])
                    th[k] = act(xh[:, k, :], vT[:, k, :], ACT.Identity, [u], bias=sc(k))
                if k > 0:
                    i = k - 1
                    tl = stt(xl[:, i, :], vT[:, i, :], sc(i), xh[:, i, :].bitcast(F32), ALU.add, ALU.subtract, [th[i]])
                    x_ready[i] = [tl]
            bfree[b] = [u]
            col_free[s_ % 2] = [tl]

        def enter(nx):
            prep(0, nx)
            prep(1, nx)
            ahead()
            for h in range(2):
                for t in range(2):
                    square(t, h)
            row_scale()
            if nx[0] == "mod":
                finish(nx)

        def leave(nx):
            if nx is not None and nx[0] == "plain":
                prep(1, nx)
                square(1, 1)
                row_scale()
                return
            square(1, 1)
            row_scale()
            if nx is not None:
                prep(1, nx)
                finish(nx)

        def add_x(t, h, b, tok, ga):
            xs = x[:, t, h * 512:(h + 1) * 512]
            if ga is None:
                r = stt(xs, ps[b], 0.5, xs, ALU.mult, ALU.add, [tok])
            elif ga == 1:
                r = tt(xs, ps[b], xs, ALU.add, [tok])
            else:
                assert len(ada_tok[ga[0]]) == 6
                r = tt(ps[b], ps[b], gaB[ga[0] % 2][:, h * 512:(h + 1) * 512], ALU.mult, [tok] + ada_tok[ga[0]])
                r = tt(xs, ps[b], xs, ALU.add, [r])
                gab_free[ga[0] % 2] = [r]
            bfree[b] = [r]
            xr[t, h] = [r]

        def into_x(label, banks2, hiT, loT, K, xw, ga, nx, hook, start=None):
            turned = nx is None
            for h in range(2):
                b, k = start[h] if start else (banks2(), 0)
                end = K if h == 0 else max(k, K - 4)
                while k < end:
                    n, td = gemm_sub(label, b, hiT, loT, k, K, xw)
                    k += n
                    hook(h, k)
                    if h == 1 and k == 4 and not turned:
                        prep(0, nx)
                        turned = True
                if h == 0:
                    for t in range(2):
                        add_x(t, h, b[t], td, ga)
                    for t in range(2):
                        square(t, 0)
                    continue
                two = [take(label) for _ in range((K - k) // 2)]
                ahead()
                for t in range(2):
                    kk = k
                    for j, hs, nk, un, tok in two:
                        for i in range(nk):
                            hi, lo = wh[hs][:, i * 512:(i + 1) * 512], wl[hs][:, i * 512:(i + 1) * 512]
                            o = ps[b[t]]
                            mm(o, hiT(kk, t), hi, kk == 0, False, [tok] + xw(kk) + (bfree[b[t]] if kk == 0 else []))
                            mm(o, hiT(kk, t), lo, False, False)
                            kk += 1
                            td = mm(o, loT(kk - 1, t), hi, False, kk == K, inc=(kk == K))
                    add_x(t, 1, b[t], td, ga)
                    if t == 0:
                        square(0, 1)
                        if not turned:
                            prep(0, nx)
                for j, *_ in two:
                    hfree[j] = td
                x_sum[0] = td
            leave(nx)

        x_sum = [None]

        sg_free = [None, None]
        hb_ready = {}
        hb_free = {}

        def ffn(label, ga, nx):
            rs = ga is None
            ring = [0]

            def banks():
                b = (ring[0] % 6, (ring[0] + 1) % 6)
                ring[0] += 2
                return b

            def turn_h(c):
                nb = 4 if c < 5 else 2
                for i in range(0, nb, 2):
                    b = next_t()
                    for ii in range(2):
                        for t in range(2):
                            tk = tr(ps[b][:, ii * 256 + t * P:ii * 256 + (t + 1) * P],
                                    hb[c % 2][t][:, (i + ii) * P:(i + ii + 1) * P],
                                    hb_ready[c] + bfree[b], inc=(ii == 1 and t == 1))
                    k = 4 * c + i
                    hi = hTh[:, k:k + 2, :].rearrange("p k s -> p (k s)")
                    lo = hTl[:, k:k + 2, :].rearrange("p k s -> p (k s)")
                    th = act(hi, ps[b], ACT.Copy, [tk])
                    tl = tt(lo, ps[b], hi.bitcast(F32), ALU.subtract, [th])
                    bfree[b] = [tl]
                    h_ready[k // 2] = [tl]
                hb_free[c] = [tk]

            h_ready = {}
            for c in range(6):
                if c < 5:
                    bg, bu = banks(), banks()
                    n, _ = gemm_sub(label + "g", bg, XH, XL, 0, 8, XW)
                    k = n
                    while k < 8:
                        n, tg = gemm_sub(label + "g", bg, XH, XL, k, 8, XW)
                        k += n
                    if c:
                        turn_h(c - 1)
                    if c == 1 and not cond_tok[0]:
                        setup_rest()
                    flush(AGE)
                    tu = gemm(label + "u", bu, XH, XL, 8, XW)
                    w = 512
                else:
                    bg = bu = banks()
                    n, _ = gemm_sub(label + "gu", bg, XH, XL, 0, 8, XW)
                    k = n
                    while k < 8:
                        n, tg = gemm_sub(label + "gu", bg, XH, XL, k, 8, XW)
                        k += n
                    tu = tg
                    turn_h(c - 1)
                    flush(AGE)
                    w = 256
                rd = []
                for t in range(2):
                    g = ps[bg[t]][:, 0:w]
                    uu = ps[bu[t]][:, 0:w] if c < 5 else ps[bu[t]][:, 256:512]
                    o = hb[c % 2][t][:, 0:w]
                    if rs:
                        r = rr[:, t:t + 1]
                        ta = act(sg[t][:, 0:w], g, ACT.Silu, [tg, sg_free[t], r_tok[0]], scale=r)
                        th = stt(o, uu, r, sg[t][:, 0:w], ALU.mult, ALU.mult, [ta, tu] + hb_free.get(c - 2, []))
                    else:
                        ta = act(sg[t][:, 0:w], g, ACT.Silu, [tg, sg_free[t]])
                        th = tt(o, uu, sg[t][:, 0:w], ALU.mult, [ta, tu] + hb_free.get(c - 2, []))
                    sg_free[t] = th
                    bfree[bg[t]] = [th]
                    bfree[bu[t]] = [th]
                    rd.append(th)
                hb_ready[c] = rd
            HH = lambda k, t: hTh[:, k, t * P:(t + 1) * P]
            HL = lambda k, t: hTl[:, k, t * P:(t + 1) * P]

            def hook(h, k):
                if h == 0 and k == 4:
                    turn_h(5)
                if k == 12:
                    flush(AGE if h == 0 else 0)
            into_x(label + "d", banks, HH, HL, 22, lambda kk: h_ready[kk // 2], ga, nx, hook)
            hb_free.clear()

        class Step:
            pass

        sbuf_free = [None, None]
        ptT_free = [None, None]
        nstep = [0]

        def attention(steps, fill):
            n = len(steps)
            for i in range(n + 2):
                for ahead_, f in ((2, 0), (1, 1)):
                    if 0 < i + ahead_ < n and steps[i + ahead_].pre is not None:
                        steps[i + ahead_].pre[f](steps[i + ahead_])
                if i < n:
                    scores(steps[i])
                    fill()
                if 0 <= i - 1 < n:
                    turn(steps[i - 1])
                    fill()
                if 0 <= i - 2:
                    values(steps[i - 2])

        def scores(st):
            n = nstep[0]
            nstep[0] += 1
            st.i = n % 2
            if st.wide:
                base, bb = 0, (4, 5)
            else:
                base, bb = 512 * (n % 2), (4 + n % 2,)
            st.tk = []
            P_ = pt_[st.i]
            for names in st.need:
                assert names in st.rdy, names
                st.w = st.w + list(st.rdy[names])
            for sgm in st.segs:
                o = sgm["o"]
                for pi, (q, k, w, m) in enumerate(sgm["parts"]):
                    free = [f for b in bb for f in bfree[b]]
                    tk = mm(s45[:, base + o:base + o + w], q, k, True, True, free + st.w, inc=True)
                    o += w
                sgm["w"] = o - sgm["o"]
            rd = []
            for sgm in st.segs:
                o, w, t = sgm["o"], sgm["w"], sgm["t"]
                d = P_[:, o:o + w]
                src = s45[:, base + o:base + o + w]
                mx = st.sm[:, t:t + 1]
                if st.fox is None:
                    m = sgm["mask"]
                    sp = d
                    if len(m.shape) == 3:
                        src = src.rearrange("p (g k) -> p g k", k=m.shape[2])
                        sp = d.rearrange("p (g k) -> p g k", k=m.shape[2])
                    if len(m.shape) == 2:
                        tm = ta = ttr(sp, src, m, mx, [tk, sbuf_free[st.i], CST])
                    else:
                        ta = tt(sp, src, m, ALU.add, [tk, sbuf_free[st.i], CST])
                        tm = red(mx, d, ALU.max, [ta])
                else:
                    ta = stt(d, src, 0.125, st.fox(t), ALU.mult, ALU.subtract, [tk, sbuf_free[st.i]] + st.foxw)
                    tm = red(mx, d, ALU.max, [ta])
                rd.append(ta)
                tn = ts(st.sm[:, 2 + t:3 + t], mx, -st.scale, None, ALU.mult, w=[tm])
                te = act(d, d, ACT.Exp, [tn], bias=st.sm[:, 2 + t:3 + t], scale=st.scale,
                         accum_out=st.sm[:, 4 + t:5 + t])
                trc = rec(st.sm[:, 6 + t:7 + t], st.sm[:, 4 + t:5 + t], [te])
                sgm["e"] = te
                sgm["r"] = trc
            for b in bb:
                bfree[b] = list(rd)

        def turn(st):
            P_, T_ = pt_[st.i], ptT[st.i]
            blocks = []
            for sgm in st.segs:
                o = sgm["o"]
                for pi, (q, k, w, m) in enumerate(sgm["parts"]):
                    for kb in range(w // P):
                        blocks.append((sgm, o, pi, kb))
                        o += P
            done = {}
            for r0 in range(0, len(blocks), 4):
                grp = blocks[r0:r0 + 4]
                for gi, (sgm, o, pi, kb) in enumerate(grp):
                    tk = tr(ps[6][:, gi * P:(gi + 1) * P], P_[:, o:o + P], [sgm["e"]] + bfree[6], inc=(gi == len(grp) - 1))
                n = len(grp) * P
                tc = act(T_[:, r0 * P:r0 * P + n], ps[6][:, 0:n], ACT.Copy, [tk, ptT_free[st.i]])
                bfree[6] = [tc]
                for gi in range(len(grp)):
                    done[r0 + gi] = tc
            sbuf_free[st.i] = tk
            st.blocks, st.turned = blocks, done

        def values(st):
            T_, blocks, done = ptT[st.i], st.blocks, st.turned
            for sgm in st.segs:
                idx = [i for i, bl in enumerate(blocks) if bl[0] is sgm]
                o = st.i * 128 + sgm["t"] * 64
                for n, i in enumerate(idx):
                    _, _, pi, kb = blocks[i]
                    tk = mm(ps[7][:, o:o + 64], T_[:, i * P:(i + 1) * P], st.v(pi, kb), n == 0, n == len(idx) - 1,
                            [done[i]] + bfree[7] + st.w, inc=(n == len(idx) - 1))
                sgm["o_ps"] = ps[7][:, o:o + 64]
            ptT_free[st.i] = tk
            rd = []
            for sgm in st.segs:
                rd.append(st.out(sgm["t"], sgm["o_ps"], st.sm[:, 6 + sgm["t"]:7 + sgm["t"]], [tk, sgm["r"]]))
            st.done = rd
            o_free[st.i] = rd
            bfree[7] = list(rd)

        o_free = [[], []]

        def pair_step(i, qT, kT, v, mask, outf, w, fox=None, foxw=(), scale=0.125, pre=None):
            st = Step()
            st.wide = False
            st.segs = [dict(t=0, o=0, parts=[(qT[:, 0:P], kT[:, 0:P], P, None)], mask=mask[:, P:2 * P] if mask is not None else None),
                       dict(t=1, o=P, parts=[(qT[:, P:S], kT[:, 0:S], S, None)], mask=mask)]
            st.v, st.out, st.w, st.fox, st.foxw, st.scale, st.pre = (lambda pi, kb: v(kb)), outf, list(w), fox, list(foxw), scale, pre
            st.need = ()
            st.sm = small[:, 8 * (i % 8):8 * (i % 8) + 8]
            return st

        def turn_heads(z, nb, dst, w, last):
            tks = []
            for b0 in range(0, nb, 2):
                b = next_t()
                n = min(2, nb - b0)
                for i in range(n):
                    for t in range(2):
                        tk = tr(ps[b][:, i * 256 + t * P:i * 256 + (t + 1) * P], z(b0 + i, t), w + bfree[b],
                                inc=(i == n - 1 and t == 1))
                r = act(dst[:, b0:b0 + n, :].rearrange("p k s -> p (k s)"), ps[b][:, 0:n * 256], ACT.Copy, [tk])
                bfree[b] = [r]
                tks.append(r)
            return tks, tk

        rt_free = [None]

        def rotate(z, cos, sin, n, half, w):
            c = cos.unsqueeze(2).broadcast_to([P, 2, n, half])
            s = sin.unsqueeze(2).broadcast_to([P, 2, n, half])
            x1, x2 = z[:, :, :, 0:half], z[:, :, :, half:2 * half]
            buf = rt1 if half > 8 else rt2
            r = [q[:, :, 0:n * half].rearrange("p t (n f) -> p t n f", f=half) for q in buf]
            w = w + [rt_free[0]]
            a = tt(r[0], x1, c, ALU.mult, w)
            b = tt(r[1], x2, s, ALU.mult, w)
            d = tt(r[2], x2, c, ALU.mult, w)
            e = tt(r[3], x1, s, ALU.mult, w)
            f = tt(x1, r[0], r[1], ALU.subtract, [a, b, e])
            g = tt(x2, r[2], r[3], ALU.add, [d, e])
            rt_free[0] = g
            return [f, g]

        zt_free = [[], []]

        ring4 = [0]

        def banks4():
            b = (ring4[0] % 4, (ring4[0] + 1) % 4)
            ring4[0] += 2
            return b

        jobs = []
        posts = []

        def job(label, done):
            jobs.append(dict(label=label, k=0, b=None, done=done))

        def fill(n=1):
            for _ in range(n):
                if not jobs and not posts:
                    return
                if jobs:
                    j = jobs[0]
                    if j["b"] is None:
                        j["b"] = banks4()
                    m, tk = gemm_sub(j["label"], j["b"], XH, XL, j["k"], 8, XW)
                    j["k"] += m
                while posts and (not jobs or posts[0][0] + LAG <= taken[0]):
                    posts.pop(0)[1]()
                if jobs and j["k"] == 8:
                    jobs.pop(0)
                    j["done"](j["b"], tk)
                flush(AGE)

        y_turned = [None]

        def turn_y(k, src, w, pos=None, dst=None):
            hd, ld = (xh, xl) if dst is None else dst
            b = next_t()
            for kk in range(2):
                for t in range(2):
                    tk = tr(ps[b][:, kk * 256 + t * P:kk * 256 + (t + 1) * P], src(k[kk], t),
                            w + bfree[b], inc=(kk == 1 and t == 1))
            hi = hd[:, pos:pos + 2, :].rearrange("p k s -> p (k s)")
            lo = ld[:, pos:pos + 2, :].rearrange("p k s -> p (k s)")
            th = act(hi, ps[b], ACT.Copy, [tk])
            tl = tt(lo, ps[b], hi.bitcast(F32), ALU.subtract, [th])
            bfree[b] = [tl]
            y_turned[0] = tk
            return [tl]

        YM = lambda k, t: ym[:, t, k * P:(k + 1) * P]
        YH = lambda k, t: yh[:, k, t * P:(t + 1) * P]
        YL = lambda k, t: yl[:, k, t * P:(t + 1) * P]

        def heads_in(b, tk, zi, rot, rs):
            z = zt[zi]
            r = []
            for t in range(2):
                r.append(act(z[:, t, 0:384], ps[b[t]][:, 0:384], ACT.Copy, [tk, r_tok[0]] + zt_free[zi],
                             scale=rr[:, t:t + 1] if rs else 1.0))
                bfree[b[t]] = [r[-1]]
            if rot is not None:
                cos, sin, half, w = rot
                r = rotate(z[:, :, 0:384].rearrange("p t (n f) -> p t n f", f=64), cos, sin, 6, half, r + w)
            return r

        def heads_out(dst, zi, r):
            z = zt[zi]
            d, tk = turn_heads(lambda i, t: z[:, t, i * P:(i + 1) * P], 3, dst, r, None)
            zt_free[zi] = [tk]
            return d

        def rows_out(dst, b, tk, w, rs, f=ACT.Copy):
            out = []
            for t in range(2):
                r = act(dst[:, t, 0:w], ps[b[t]][:, 0:w], f, [tk, r_tok[0]], scale=rr[:, t:t + 1] if rs else 1.0)
                bfree[b[t]] = [r]
                out.append(r)
            return out

        def mix1(l, nx):
            rdy = {}
            conv = dict(k=0, tok=None)

            def taps(n):
                if conv["tok"] is None:
                    return
                for k in range(conv["k"], min(conv["k"] + n, 31)):
                    for c in range(2):
                        wc = cols2[:, (2 * l + c) * 31 + k:(2 * l + c) * 31 + k + 1]
                        src = upad[:, c, k:k + 256]
                        if k == 0:
                            tk = ts(cacc[:, c, :], src, wc, cols2[:, 124 + 2 * l + c:125 + 2 * l + c], ALU.mult, ALU.add,
                                    w=conv["tok"][c])
                        else:
                            tk = stt(cacc[:, c, :], src, wc, cacc[:, c, :], ALU.mult, ALU.add, conv["tok"][c])
                        conv["tok"][c] = [tk]
                conv["k"] = min(conv["k"] + n, 31)

            def c_done(b, tk):
                tz_ = DV.put(lambda e: e.memset(upad[:, :, 0:32], 0.0), [tk])
                for t in range(2):
                    r = rr[:, t:t + 1]
                    sgm = zt[0][:, t, 0:256]
                    ta = act(sgm, ps[b[t]][:, 256:512], ACT.Sigmoid, [tk, r_tok[0]] + zt_free[0], scale=r)
                    tu = stt(zt[1][:, t, 0:256], ps[b[t]][:, 0:256], r, sgm, ALU.mult, ALU.mult, [ta] + zt_free[1])
                    bfree[b[t]] = [tu]
                zt_free[0] = [tu]

                def post():
                    b = next_t()
                    for c in range(2):
                        for t in range(2):
                            tk = tr(ps[b][:, c * 256 + t * P:c * 256 + (t + 1) * P], zt[1][:, t, c * P:(c + 1) * P],
                                    [tu] + bfree[b], inc=(c == 1 and t == 1))
                    zt_free[1] = [tk]
                    tp = act(upad[:, :, 30:286], ps[b].rearrange("p (c s) -> p c s", c=2), ACT.Copy, [tk, tz_])
                    bfree[b] = [tp]
                    conv["tok"] = [[tp], [tp]]
                posts.append((taken[0], post))

            def q_done(n, zi, rot):
                def done(b, tk):
                    r = heads_in(b, tk, zi, rot, True)

                    def post():
                        rdy[n] = heads_out(qk1[n], zi, r)
                    posts.append((taken[0], post))
                return done

            def v_done(n, dst, f=ACT.Copy):
                def done(b, tk):
                    rdy[n] = rows_out(dst, b, tk, 384, True, f)
                return done

            rope = (cos1[:, :, 32:40], sin1[:, :, 32:40], 8, [TRIG[0]])
            ret = (cos1[:, :, 0:32], sin1[:, :, 0:32], 32, [TRIG[0]])
            job("c", c_done)
            job("mq", q_done("mq", 0, rope))
            job("mk", q_done("mk", 1, rope))
            job("mv", v_done("mv", mv))
            job("rq", q_done("rq", 0, ret))
            job("rk", q_done("rk", 1, ret))
            job("rv", v_done("rv", rv))
            job("rg", v_done("rg", rg, ACT.Silu))
            for i in range(16):
                fill()
                taps(2 if i > 6 else 0)

            def step_fill():
                fill()
                taps(1)

            steps = []
            for h in range(6):
                lo_ = 64 * (h % 2)
                qT = qk1["mq"][lo_:lo_ + 64, h // 2, :]
                kT = qk1["mk"][lo_:lo_ + 64, h // 2, :]

                def outf(t, o, r, w, h=h):
                    return ts(ym[:, t, 384 + 64 * h:448 + 64 * h], o, r, None, ALU.mult, w=w)
                steps.append(pair_step(h, qT, kT, lambda kb, h=h: mv[:, kb, 64 * h:64 * h + 64], causal, outf,
                                       rdy["mq"] + rdy["mk"] + rdy["mv"]))
            attention(steps, step_fill)
            ymoba = [r for st in steps for r in st.done]

            tks = {}
            yr = zt[1][:, :, 0:384]
            srg = rg
            yret, rdo, last_y = {}, [], [None]

            def pair_norm(j):
                c = slice(128 * j, 128 * j + 128)
                sqv = ym[:, :, c]
                sm0, sm1, sm2 = (small[:, 64 + 12 * i + 4 * j:68 + 12 * i + 4 * j] for i in range(3))
                a = tt(sqv, yr[:, :, c], yr[:, :, c], ALU.mult, rdo)
                a = red(sm0.rearrange("p (t h) -> p t h", t=2), sqv.rearrange("p t (h e) -> p t h e", e=64), ALU.add, [a])
                a = ts(sm1, sm0, 1.0 / 64, EPS, ALU.mult, ALU.add, w=[a])
                a = tt(sm2, sm1, phalf[:, 0:1].broadcast_to([P, 4]), ALU.pow, [a], L=PO)
                z = tt(srg[:, :, c], srg[:, :, c], yr[:, :, c], ALU.mult, rdy["rg"] + rdo)
                rb = sm2.rearrange("p (t h) -> p t h", t=2).unsqueeze(3).broadcast_to([P, 2, 2, 64])
                yret[j] = tt(sqv.rearrange("p t (h e) -> p t h e", e=64),
                             srg[:, :, c].rearrange("p t (h e) -> p t h e", e=64), rb, ALU.mult, [a, z])
                last_y[0] = z

            def conv_turn():
                b = next_t()
                for c in range(2):
                    for t in range(2):
                        tk = tr(ps[b][:, c * 256 + t * P:c * 256 + (t + 1) * P], cacc[:, c, t * P:(t + 1) * P],
                                conv["tok"][0] + conv["tok"][1] + bfree[b], inc=(c == 1 and t == 1))
                pv = ps[b].rearrange("p (c t s) -> p t c s", c=2, t=2)
                r = act(yc[:, :, :].rearrange("p t (c s) -> p t c s", c=2), pv, ACT.Copy, [tk])
                bfree[b] = [r]
                return r

            def conv_norm(r):
                y4 = yc[:, :, :].rearrange("p t (g e) -> p t g e", e=64)
                z4 = yc2[:, :, :].rearrange("p t (g e) -> p t g e", e=64)
                s0, s1, s2 = small[:, 104:112], small[:, 112:120], small[:, 120:128]
                three = lambda s: s.rearrange("p (t g) -> p t g", t=2)
                bc = lambda s: three(s).unsqueeze(3).broadcast_to([P, 2, 4, 64])
                a = red(three(s0), y4, ALU.add, [r])
                yield a
                a = ts(s0, s0, 1.0 / 64, None, ALU.mult, w=[a])
                a = tt(y4, y4, bc(s0), ALU.subtract, [a])
                yield a
                q = tt(z4, y4, y4, ALU.mult, [a])
                yield q
                q = red(three(s1), z4, ALU.add, [q])
                q = ts(s1, s1, 1.0 / 64, EPS, ALU.mult, ALU.add, w=[q])
                q = tt(s2, s1, phalf[:, 0:1].broadcast_to([P, 8]), ALU.pow, [q], L=PO)
                yield q
                a = tt(y4, y4, bc(s2), ALU.mult, [a, q])
                yield a
                y2 = yc[:, :, :]
                a = tt(y2, y2, lngb[:, l, 0, :].unsqueeze(1).broadcast_to([P, 2, 256]), ALU.mult, [a, MISC])
                yield a
                a = tt(y2, y2, lngb[:, l, 1, :].unsqueeze(1).broadcast_to([P, 2, 256]), ALU.add, [a])
                yield act(ym[:, :, 768:1024], y2, ACT.Silu, [a])

            taps(31)
            ytok = {}
            d_ = (y1h, y1l)
            YH1 = lambda k, t: y1h[:, k, t * P:(t + 1) * P]
            YL1 = lambda k, t: y1l[:, k, t * P:(t + 1) * P]
            wo_b, wo_n = [banks4(), banks4()], [0]

            yconv = [None]
            wo_y = [((3, 4), lambda: ymoba + [rt_free[0]] + conv["tok"][0] + conv["tok"][1]),
                    ((5, 6), lambda: ymoba + [a for a in cn] + yconv), ((7, 0), lambda: [yret[0]] + yconv),
                    ((1, 2), lambda: [yret[1], yret[2]])]

            def turn_wo(i):
                tiles, w = wo_y[i]
                ytok[i] = turn_y(tiles, YM, w(), 2 * i, d_)

            def step():
                if jobs or posts:
                    fill()
                elif wo_n[0] < 4:
                    k0, half = divmod(wo_n[0], 2)
                    if half:
                        turn_wo(k0 + 1)
                    gemm_sub("wo", wo_b[half], YH1, YL1, 2 * k0, 8, lambda k: ytok[k // 2])
                    wo_n[0] += 1

            rfree = {i: sbuf_free[i % 2] for i in range(4)}
            for h in range(8):
                if h < 6:
                    n = nstep[0]
                    nstep[0] += 1
                    b, si_ = 4 + n % 2, h % 4
                    lo_ = 64 * (h % 2)
                    qT = qk1["rq"][lo_:lo_ + 64, h // 2, :]
                    kT = qk1["rk"][lo_:lo_ + 64, h // 2, :]
                    mm(ps[b][:, 0:256], kT[:, 0:P], qT[:, 0:256], True, True, bfree[b] + rdy["rq"] + rdy["rk"])
                    tk = mm(ps[b][:, 256:384], kT[:, P:S], qT[:, P:S], True, True, inc=True)
                    d = pt_[si_ % 2][:, 384 * (si_ // 2):384 * (si_ // 2) + 384]
                    tt(d[:, 0:256], ps[b][:, 0:256], decay[:, h, :], ALU.mult, [tk, rfree[si_], CST])
                    t2 = tt(d[:, 256:384], ps[b][:, 256:384], decay[:, h, 0:P], ALU.mult, [tk])
                    bfree[b] = [t2]
                    tks[h] = (si_, d, t2)
                if h > 1:
                    hh = h - 2
                    si_, d, t2 = tks[hh]
                    v = lambda kb: rv[:, kb, 64 * hh:64 * hh + 64]
                    mm(ps[7][:, 0:64], d[:, 0:P], v(0), True, True, [t2] + bfree[7] + rdy["rv"])
                    mm(ps[7][:, 64:128], d[:, P:S], v(0), True, False)
                    tk = mm(ps[7][:, 64:128], d[:, S:S + P], v(1), False, True, inc=True)
                    rfree[si_] = tk
                    r = act(yr[:, :, 64 * hh:64 * hh + 64], ps[7][:, 0:128].rearrange("p (t e) -> p t e", t=2),
                            ACT.Copy, [tk] + zt_free[1])
                    bfree[7] = [r]
                    rdo.append(r)
                step()
                if h > 2 and h % 2:
                    while "rg" not in rdy:
                        fill()
                    pair_norm((h - 3) // 2)
                if h == 0:
                    rc = conv_turn()
                    turn_wo(0)
                    cn = conv_norm(rc)
                else:
                    for _ in range(2):
                        yconv[0] = next(cn, yconv[0])
            while wo_n[0] < 4:
                step()
            sbuf_free[0] = sbuf_free[1] = tk
            zt_free[0], zt_free[1] = [last_y[0]], [last_y[0]]
            gemm_sub("wo", wo_b[0], YH1, YL1, 4, 8, lambda k: ytok[k // 2])
            turn_wo(3)
            gemm_sub("wo", wo_b[1], YH1, YL1, 4, 8, lambda k: ytok[k // 2])
            into_x("wo", None, YH1, YL1, 8, lambda k: ytok[k // 2], 1, nx, lambda h, k: None,
                   [(wo_b[h], 6) for h in range(2)])

        def mix2(l, s_, nx):
            rdy = {}
            kdr = {}

            def n0_done(b, tk):
                z = zt[0]
                r = []
                for t in range(2):
                    r.append(act(z[:, t, :], ps[b[t]], ACT.Copy, [tk] + zt_free[0]))
                    bfree[b[t]] = [r[-1]]
                zq = z[:, :, 0:256].rearrange("p t (n f) -> p t n f", f=64)
                zk = z[:, :, 256:512].rearrange("p t (n f) -> p t n f", f=128)
                rdy["n0"] = r
                rdy["ro"] = rotate(zq, cos2, sin2, 4, 8, r + [CST]) + rotate(zk, cos2, sin2, 2, 8, r)

            def n1_done(b, tk):
                z, z1 = zt[0], zt[1]
                r1 = []
                for t in range(2):
                    r1.append(act(z1[:, t, 0:140], ps[b[t]][:, 0:140], ACT.Copy, [tk] + zt_free[1]))
                    bfree[b[t]] = [r1[-1]]
                ro1 = rotate(z1[:, :, 0:64].rearrange("p t (n f) -> p t n f", f=64), cos2, sin2, 1, 8, r1)

                def twice(j, src):
                    return cp(dup[:, :, j, :].rearrange("p t (a f) -> p t a f", a=2),
                              src.unsqueeze(2).broadcast_to([P, 2, 2, 64]), rdy["ro"] + ro1)
                td = [twice(0, z[:, :, 256:320]), twice(1, z[:, :, 320:384]), twice(2, z[:, :, 384:448]),
                      twice(3, z1[:, :, 0:64])]
                rv_ = [cp(vn[:, :, 0, :], z[:, :, 448:512], rdy["n0"]), cp(vn[:, :, 1, :], z1[:, :, 64:128], r1)]
                rdy["vn"] = rv_
                tg = cp(ng[:, :, :], z1[:, :, 128:140], r1)
                rdy["sgn"] = act(ng[:, :, :], ng[:, :, :], ACT.Sigmoid, [tg])
                zt_free[1] = [tg]

                def post():
                    tks, tkq = turn_heads(lambda i, t: z[:, t, i * P:(i + 1) * P], 2, qn, rdy["ro"], None)
                    rdy["qn"] = tks
                    zt_free[0] = [tg, tkq]
                    for j in range(4):
                        b = next_t()
                        for t in range(2):
                            tk = tr(ps[b][:, t * P:(t + 1) * P], dup[:, t, j, :], td + bfree[b], inc=(t == 1))
                        if j < 2:
                            a1 = act(kd[0:64, j, :], ps[b][0:64, 0:256], ACT.Copy, [tk])
                            a2 = act(kd[64:128, j, 0:255], ps[b][64:128, 1:256], ACT.Copy, [tk])
                            kdr[j] = [a1, a2]
                        else:
                            kdr[j] = [act(kd[:, j, :], ps[b][:, 0:256], ACT.Copy, [tk])]
                        bfree[b] = kdr[j]
                    sbuf_free[0] = sbuf_free[1] = tk
                posts.append((taken[0], post))

            rope2 = (cos2, sin2, 8, [CST])

            def q_done(n, zi, rot):
                def done(b, tk):
                    r = heads_in(b, tk, zi, rot, False)

                    def post():
                        rdy[n] = heads_out(qk2[n], zi, r)
                    posts.append((taken[0], post))
                return done

            def dv_done(b, tk):
                rdy["dv"] = rows_out(vd, b, tk, 384, False)

            def fv_done(b, tk):
                out = []
                for t in range(2):
                    act(vf[:, t, :], ps[b[t]][:, 0:384], ACT.Copy, [tk])
                    r = act(logf[:, t, :], ps[b[t]][:, 384:390], ACT.Copy, [tk])
                    bfree[b[t]] = [r]
                    out.append(r)
                rdy["fv"] = out
                fb = small[:, 208:214]
                dma(SP, fb, A["fox_f_bias_2"][l].partition_broadcast(P), s_fin[0], fb_free[0])
                n_fin[0] += 16
                lf = logf[:, :, :]
                a = tt(lf, lf, fb.unsqueeze(1).broadcast_to([P, 2, 6]), ALU.add, out + [(s_fin[0], n_fin[0])])
                fb_free[0] = [a]
                ab = small[:, 216:228].rearrange("p (t h) -> p t h", t=2)
                a1 = stt(ab, lf, -1.0, lf, ALU.mult, ALU.max, [a])
                a1 = act(ab, ab, ACT.Exp, [a1], scale=-1.0)
                a1 = act(ab, ab, ACT.Ln, [a1], bias=1.0)
                a2 = ts(lf, lf, 0.0, None, ALU.min, w=[a, a1])
                LF = tt(lf, lf, ab, ALU.subtract, [a2, a1])
                rdy["LF"] = LF

                def post():
                    b = next_t()
                    mm(ps[b][:, 0:6], tri[:, 0:P], logf[:, 0, :], True, True, [LF] + bfree[b])
                    mm(ps[b][:, 8:14], tri[:, P:S], logf[:, 0, :], True, False)
                    tk = mm(ps[b][:, 8:14], tri[:, 0:P], logf[:, 1, :], False, True, inc=True)
                    cqt = cp(cq[:, :, :], ps[b][:, 0:16].rearrange("p (t n) -> p t n", t=2)[:, :, 0:6], [tk])
                    bfree[b] = [cqt]
                    rdy["cq"] = cqt
                posts.append((taken[0], post))

            gtok = {}

            def mg_done(i):
                br, hf = divmod(i, 2)

                def done(b, tk):
                    for t in range(2):
                        r = act(gts[:, t, br, 512 * hf:512 * hf + 512], ps[b[t]], ACT.Copy, [tk] + w1_free)
                        bfree[b[t]] = [r]
                        gtok[br, hf, t] = r
                return done

            direct, w1_free = [], []
            for kv in range(2):
                dma(SP, w1b[kv][:, :].rearrange("p (j n) -> p j n", n=128),
                    A["nsa_cmp_w1_2"][l, kv].rearrange("(j p) n -> p j n", p=P), s_w1[kv], [x_sum[0]])
                n_w1[kv] += 16
                direct.append((s_w1[kv], n_w1[kv]))

            job("n0", n0_done)
            job("n1", n1_done)
            job("dq", q_done("dq", 0, rope2))
            job("dk", q_done("dk", 1, rope2))
            fill(6)
            job("dv", dv_done)
            job("fq", q_done("fq", 0, None))
            job("fk", q_done("fk", 1, None))
            job("fv", fv_done)
            for i in range(6):
                job("mg", mg_done(i))
            while "qn" not in rdy:
                fill()

            hid = small[:, 128:192].rearrange("p (v n) -> p v n", v=2)
            blk = ptT[0][:, 0:240].rearrange("p (j n) -> p j n", j=16)
            blv = ptT[1][:, 0:240].rearrange("p (j n) -> p j n", j=16)
            hs_tok, hr_tok = [], []
            tz_ = DV.put(lambda e: e.memset(small[:, 128:192], 0.0), [])
            bw = []
            for kv, bk in ((0, blk), (1, blv)):
                pe_ = cols3[:, (2 * l + kv) * 16:(2 * l + kv) * 16 + 16].unsqueeze(2)
                ap = kd[:, kv, 0:256].rearrange("p (n j b) -> p j n b", b=2, j=8)[:, :, :, 0]
                ta = tt(bk[:, 0:8, :], ap[:, :, 0:15], pe_[:, 0:8, :].broadcast_to([P, 8, 15]), ALU.add,
                        kdr[kv] + [ptT_free[kv]])
                tb2 = tt(bk[:, 8:16, :], ap[:, :, 1:16], pe_[:, 8:16, :].broadcast_to([P, 8, 15]), ALU.add, [])
                bw.append([ta, tb2])
            for kv, bk in ((0, blk), (1, blv)):
                tok = direct[kv]
                wv = w1b[kv][:, :].rearrange("p (j n) -> p j n", n=128)
                b = next_t()
                for jj in range(16):
                    tk = mm(ps[b][0:15, 0:P], bk[:, jj, :], wv[:, jj, :], jj == 0, jj == 15, [tok] + bw[kv] + bfree[b],
                            inc=(jj == 15))
                ptT_free[kv] = tk
                w1_free.append(tk)
                hr = pt_[kv][0:15, 512:640]
                r = act(hr, ps[b][0:15, 0:P], ACT.Silu, [tk, sbuf_free[kv]])
                bfree[b] = [r]
                hr_tok.append((hr, r))
                fill()
            b = next_t()
            for kv in range(2):
                hr, r = hr_tok[kv]
                tk = tr(ps[b][:, 16 * kv:16 * kv + 15], hr, [r] + bfree[b], inc=True)
            r = act(hid[:, :, 0:15], ps[b][:, 0:32].rearrange("p (v n) -> p v n", v=2)[:, :, 0:15], ACT.Copy, [tk, tz_])
            bfree[b] = [r]
            hrep = ptT[0][:, 256:384].rearrange("p (h n) -> p h n", h=4)
            rr_ = cp(hrep, hid[:, 1, :].unsqueeze(1).broadcast_to([P, 4, 32]), [r])
            vbd = ptT[1][:, 256:512]
            tzz = DV.put(lambda e: e.memset(vbd, 0.0), [ptT_free[1]])
            fill()
            b = next_t()
            kcT = small[:, 192:208]
            mm(ps[b][:, 0:15], w2d[:, l, 0:2, :].rearrange("p a f -> p (a f)"), hid[:, 0, 0:15], True, True,
               [r, MISC] + bfree[b])
            tk = mm(ps[b][:, 64:128], ptT[0][:, 256:384], w2d[:, l, 2, :], True, True, [rr_], inc=True)
            KC = [cp(kcT[:, 0:15], ps[b][:, 0:15], [tk])]
            vb = []
            for h in range(4):
                vb.append(cp(vbd[32 * h:32 * h + 32, 64 * h:64 * h + 64], ps[b][32 * h:32 * h + 32, 64:128], [tk, tzz]))
            bfree[b] = list(vb)
            fill()

            for h in (0, 2, 1, 3):
                lo_, b = 64 * (h % 2), 4 + h % 2
                for t in range(2):
                    o = 32 * t + 16 * (h // 2)
                    tk = mm(ps[b][:, o:o + 15], qn[lo_:lo_ + 64, h // 2, t * P:(t + 1) * P],
                            kcT[lo_:lo_ + 64, 0:15], True, True, KC + rdy["qn"] + bfree[b], inc=True)
            pc = pt_[0][:, 0:256].rearrange("p (t h n) -> p t h n", t=2, h=4)
            p15 = pc[:, :, :, 0:15]
            tzz = DV.put(lambda e: e.memset(pt_[0][:, 0:256], 0.0), [sbuf_free[0]])
            cm_ = C("cmpm").rearrange("p (t n) -> p t n", t=2)
            c01 = C("cmp01").rearrange("p (t n) -> p t n", t=2)
            a = []
            for par in range(2):
                sv = ps[4 + par][:, 0:64].rearrange("p (t h n) -> p t h n", t=2, h=2)[:, :, :, 0:15]
                for t in range(2):
                    a.append(tt(p15[:, t, par::2], sv[:, t], cm_[:, t].unsqueeze(1).broadcast_to([P, 2, 15]), ALU.add,
                                [tk, tzz]))
                bfree[4 + par] = [a[-1]]
            mb = small[:, 64:72].rearrange("p (t h) -> p t h", t=2)
            m = red(mb, p15, ALU.max, a)
            a = []
            for t in range(2):
                a.append(tt(p15[:, t], p15[:, t], mb[:, t].unsqueeze(2).broadcast_to([P, 4, 15]), ALU.subtract, [m]))
            e_ = act(p15, p15, ACT.Exp, a, scale=0.125)
            fill()
            a = []
            for t in range(2):
                a.append(tt(p15[:, t], p15[:, t], c01[:, t].unsqueeze(1).broadcast_to([P, 4, 15]), ALU.mult, [e_]))
            dn = small[:, 72:80]
            db = dn.rearrange("p (t h) -> p t h", t=2)
            m = red(db, p15, ALU.add, a)
            m = ts(dn, dn, 1e-30, None, ALU.max, w=[m])
            m = rec(dn, dn, [m])
            a = []
            for t in range(2):
                a.append(tt(p15[:, t], p15[:, t], db[:, t].unsqueeze(2).broadcast_to([P, 4, 15]), ALU.mult, [m]))
            fill()
            for t in range(2):
                tk = tr(ps[6][:, t * P:(t + 1) * P], pt_[0][:, t * P:(t + 1) * P], a + bfree[6], inc=(t == 1))
            sbuf_free[0] = tk
            pT = ptT[0][:, 384:640]
            r = act(pT, ps[6][:, 0:256], ACT.Copy, [tk])
            bfree[6] = [r]
            fill()
            for t in range(2):
                tk = mm(ps[7][:, t * 256:(t + 1) * 256], pT[:, t * P:(t + 1) * P], vbd, True, True, [r] + vb + bfree[7],
                        inc=(t == 1))
            ptT_free[0] = ptT_free[1] = tk
            gv = ng[:, :, :].rearrange("p t (h c) -> p t h c", c=3)
            cm1 = []
            for t in range(2):
                cm1.append(tt(ym[:, t, 0:256].rearrange("p (h e) -> p h e", e=64),
                              ps[7][:, t * 256:(t + 1) * 256].rearrange("p (h e) -> p h e", e=64),
                              gv[:, t, :, 0:1].broadcast_to([P, 4, 64]), ALU.mult, [tk, rdy["sgn"]]))
            bfree[7] = list(cm1)
            ycur = {(t, h): cm1 for t in range(2) for h in range(4)}

            steps = []
            for which in range(2):
                for h in range(4):
                    lo_ = 64 * (h % 2)

                    def outf(t, o, r, w, h=h, which=which):
                        f = small[:, 80 + t:81 + t]
                        a = tt(f, r, ng[:, t, 3 * h + 1 + which:3 * h + 2 + which], ALU.mult, w)
                        yy = ym[:, t, 64 * h:64 * h + 64]
                        q = stt(yy, o, f, yy, ALU.mult, ALU.add, [a] + ycur[t, h])
                        ycur[t, h] = [q]
                        return q
                    steps.append(pair_step(len(steps), qn[lo_:lo_ + 64, h // 2, :], kd[lo_:lo_ + 64, 2 + which, :],
                                           lambda kb, which=which: vn[:, kb, which, :], causal, outf,
                                           rdy["qn"] + kdr[2 + which] + rdy["vn"]))
            nnsa = len(steps)

            for h in range(2):
                for t in range(2):
                    st = Step()
                    st.wide = t == 1
                    w = P * (t + 1)
                    parts = []
                    for g in range(3):
                        hh = 2 * g + h
                        lo_ = 64 * (hh % 2)
                        parts.append((qk2["dq"][lo_:lo_ + 64, hh // 2, t * P:(t + 1) * P],
                                      qk2["dk"][lo_:lo_ + 64, hh // 2, 0:w], w, None))
                    mk = masks.rearrange("p g b k -> p g (b k)")
                    st.segs = [dict(t=t, o=0, parts=parts, mask=mk[:, :, P:2 * P] if t == 0 else mk)]
                    st.v = lambda pi, kb, h=h: vd[:, kb, 64 * (2 * pi + h):64 * (2 * pi + h) + 64]
                    st.out = lambda t, o, r, w, h=h: ts(ym[:, t, 256 + 64 * h:320 + 64 * h], o, r, None, ALU.mult, w=w)
                    st.w, st.fox, st.foxw, st.scale = [], None, [], 0.125
                    st.pre, st.need, st.rdy = None, ("dq", "dk", "dv"), rdy
                    st.sm = small[:, 8 * (len(steps) % 8):8 * (len(steps) % 8) + 8]
                    steps.append(st)
            ndil = len(steps)
            fbuf = [zt[i][:, :, :].rearrange("p t n -> p (t n)") for i in range(2)]
            ffree = {}

            for h in range(6):
                lo_ = 64 * (h % 2)
                fz_ = fbuf[h % 2]
                lb = fz_[:, 0:256].rearrange("p (t q) -> p t q", t=2)
                fm = fz_[:, 256:640]
                stp = pair_step(len(steps), qk2["fq"][lo_:lo_ + 64, h // 2, :], qk2["fk"][lo_:lo_ + 64, h // 2, :],
                                lambda kb, h=h: vf[:, kb, 64 * h:64 * h + 64], None,
                                lambda t, o, r, w, h=h: ts(ym[:, t, 384 + 64 * h:448 + 64 * h], o, r, None, ALU.mult, w=w),
                                [], scale=1.0)

                def pre0(st, h=h, lb=lb):
                    st.lb = [act(lb[:, t, :], ones, ACT.Copy, [rdy["LF"]] + ffree.get(h - 2, zt_free[h % 2]),
                                 scale=logf[:, t, h:h + 1]) for t in range(2)]

                def pre1(st, h=h, lb=lb, fm=fm):
                    b = next_t()
                    mm(ps[b][:, 0:256], lb[:, 0, :], tri[:, 0:256], True, False, st.lb + bfree[b])
                    tk = mm(ps[b][:, 128:256], lb[:, 1, :], tri[:, 0:P], False, True, inc=True)
                    b1 = stt(fm[:, 0:P], ps[b][:, 0:P], cq[:, 0, h:h + 1], causal[:, P:2 * P], ALU.subtract, ALU.subtract,
                             [tk, rdy["cq"]])
                    b2 = stt(fm[:, P:3 * P], ps[b][:, 0:256], cq[:, 1, h:h + 1], causal, ALU.subtract, ALU.subtract, [tk])
                    bfree[b] = [b2]
                    st.foxw = [b1, b2]
                    ffree[h] = [b2]
                stp.pre, stp.need, stp.rdy = (pre0, pre1), ("fq", "fk", "fv"), rdy
                stp.fox = lambda t, fm=fm: fm[:, 0:P] if t == 0 else fm[:, P:3 * P]
                steps.append(stp)
            attention(steps, fill)
            while jobs or posts:
                fill()
            zt_free[0] = zt_free[1] = list(steps[-1].done)
            dn_ = lambda a, b: [r for st in steps[a:b] for r in st.done]
            sgt = {}

            def gates(hf):
                for br in range(3):
                    for t in range(2):
                        g = gts[:, t, br, 512 * hf:512 * hf + 512]
                        sgt[br, hf, t] = act(g, g, ACT.Sigmoid, [gtok[br, hf, t]])
            x_ready[0] = x_ready[1] = turn_y((0, 1), YM, dn_(0, nnsa), 0)
            x_ready[2] = x_ready[3] = turn_y((2, 3), YM, dn_(nnsa, ndil + 2), 2)
            x_ready[4] = x_ready[5] = turn_y((4, 5), YM, dn_(ndil + 2, len(steps)), 4)
            gates(0)
            ym_free = y_turned[0]
            mrg = {}
            yt = {}
            d = (yh, yl)
            for hf in range(2):
                banks = [(0, 1), (2, 3), (4, 5)]
                kpos = 0
                w = [mrg[t] for t in mrg]
                a = {}
                br = [(0, 0, 2), (0, 1, 2), (1, 0, 1), (2, 0, 3), (2, 1, 3), (2, 2, 3)]
                while kpos < 6:
                    j, hs, nk, un, tok = take("br")
                    for k in range(nk):
                        kk = kpos + k
                        bi, ki, kn = br[kk]
                        hi, lo = wh[hs][:, k * 512:(k + 1) * 512], wl[hs][:, k * 512:(k + 1) * 512]
                        for t in range(2):
                            bb = banks[bi][t]
                            ww = [tok] + XW(kk) + (bfree[bb] if ki == 0 else [])
                            mm(ps[bb], XH(kk, t), hi, ki == 0, False, ww)
                            mm(ps[bb], XH(kk, t), lo, False, False)
                            tk = mm(ps[bb], XL(kk, t), hi, False, ki == kn - 1, inc=(t == 1))
                    hfree[j] = tk
                    kpos += nk
                    if kpos == 2 and hf == 0:
                        gates(1)
                    if ki == kn - 1:
                        for t in range(2):
                            g = lambda n: gts[:, t, n, 512 * hf:512 * hf + 512]
                            a[bi, t] = tt(g(bi), ps[banks[bi][t]], g(bi), ALU.mult, [tk, sgt[bi, hf, t]])
                            bfree[banks[bi][t]] = [a[bi, t]]
                            if bi == 1:
                                a[1, t] = tt(g(0), g(0), g(1), ALU.add, [a[0, t], a[1, t]])
                            elif bi == 2:
                                mrg[t] = tt(ym[:, t, 512 * hf:512 * hf + 512], g(0), g(2), ALU.add,
                                            [a[1, t], a[2, t], ym_free])
                    ahead()
                    if hf and kpos == 3:
                        w = w + [sbuf_free[0], sbuf_free[1], ptT_free[0], ptT_free[1]]
                        yt[0] = turn_y((0, 1), YM, w, 0, d)
                    if hf and kpos == 5:
                        yt[1] = turn_y((2, 3), YM, w, 2, d)
            w2b = [banks4(), banks4()]
            for h in range(2):
                for k in (0, 2):
                    gemm_sub("wo2", w2b[h], YH, YL, k, 8, lambda k: yt[k // 2])
            w = [mrg[0], mrg[1]]
            yt[2] = turn_y((4, 5), YM, w, 4, d)
            yt[3] = turn_y((6, 7), YM, w, 6, d)
            flush()
            into_x("wo2", None, YH, YL, 8, lambda k: yt[k // 2], (s_,), nx, lambda h, k: flush(0 if k == 8 else AGE),
                   [(w2b[h], 4) for h in range(2)])

        fb_free = [[]]
        n_w1 = [0, 0]
        n_fin = [0, 0]

        def final(gb, w, dst):
            for h in range(2):
                for t in range(2):
                    c = slice(512 * h, 512 * h + 512)
                    rd = stt(dst[:, t, c], x[:, t, c], rr[:, t:t + 1], gb[:, c], ALU.mult, ALU.mult, [r_tok[0]] + w)
                    xr[t, h] = [rd]
            return rd

        def plain(o):
            return ("plain", lambda k: cols1[:, o + k:o + k + 1], [g1])

        plan = SUBS[:stop] if stop < 99 else SUBS
        norms = [plain(o) for o in (0, 16, 32, 8, 24, 40)] + [("mod", i) for i in range(6)]
        enter(norms[0])
        for si, kind in enumerate(plan):
            l = (si // 3) % 2
            nx = None if si in (5, 11) or si + 1 == len(plan) else norms[si + 1]
            s_ = si - 6
            if si == 5:
                dma(SP, gaB[1][:, :], A["final_norm"].partition_broadcast(P), s_fin[1])
            elif si == 11:
                dma(SP, gaB[0][:, :], A["final_norm_g_2"].partition_broadcast(P), s_fin[1], gab_free[0])
            if si in (5, 11):
                n_fin[1] += 16
            if kind in ("f1", "f2"):
                ffn(kind, None, nx)
            elif kind == "m":
                mix1(l, nx)
            elif kind == "M":
                mix2(l, s_, nx)
            else:
                ffn(kind, (s_,), nx)
            if si == 5:
                gab_free[1] = [final(gaB[1][:, :], [(s_fin[1], n_fin[1])], x)]
                if len(plan) > 6:
                    enter(norms[6])
        if stop >= 12:
            rd = final(gaB[0][:, :], [(s_fin[1], n_fin[1])], x)
        for h in range(2):
            for t in range(2):
                c = slice(512 * h, 512 * h + 512)
                dma(SP, out[0, t * P:(t + 1) * P, c], x[:, t, c], s_out, xr[t, h])
        SP.put(None, [(s_out, 64), MISC] + bt_all, False)

        block = ctx.enter_context(nc.Block())

        @block.sync
        def _(e):
            SP.play(e)

        @block.scalar
        def _(e):
            AC.play(e)

        @block.vector
        def _(e):
            DV.play(e)

        @block.gpsimd
        def _(e):
            PO.play(e)

        @block.tensor
        def _(e):
            PE.play(e)


_INS = ["x", "positions", "ffn1_norm", "ffn1_wg", "ffn1_wu", "ffn1_wd", "mix_norm", "w_in", "conv_w", "conv_b",
        "conv_ln_g", "conv_ln_b", "w_out", "ffn2_norm", "ffn2_wg", "ffn2_wu", "ffn2_wd", "final_norm", "c_2",
        "ada_w_2", "ada_b_2", "norm_g_2", "final_norm_g_2", "ffn_w_in_2", "ffn_w_out_2", "mix_w_in_2",
        "nsa_cmp_pe_2", "nsa_cmp_w1_2", "nsa_cmp_w2_2", "fox_f_bias_2", "br_w_nsa_2", "br_w_dil_2", "br_w_fox_2",
        "mix_w_out_2"]


def kernel(**inputs):
    import concourse.bacc as _bacc
    from concourse.bass_utils import run_bass_kernel_spmd as _run

    nc = _bacc.Bacc("TRN2", target_bir_lowering=False, num_devices=1)
    arrays, A = {}, {}
    given = {n: np.ascontiguousarray(inputs[n]) for n in _INS}
    given["cst"] = constants()
    for name, a in given.items():
        arrays[f"in_{name}"] = a
        A[name] = nc.dram_tensor(f"in_{name}", a.shape, mybir.dt.from_np(a.dtype), kind="ExternalInput").ap()
    out = nc.dram_tensor("out_0", (1, S, D), F32, kind="ExternalOutput").ap()
    program(nc, A, out)
    r = _run(nc, [arrays], core_ids=[0])
    return r.results[0]["out_0"]
```
